# Optimizing a Trainium2 kernel written in Bass

```python
import jax
import jax.numpy as jnp
from jax import lax
import numpy as np

D_MODEL = 1024
BATCH = 1
SEQ = 1024
DEPTH = 1
DEC_BATCH = 8
DEC_SEQ = 4
PAST_LEN = 512
PAGE_SIZE = 128

H_M = 4
DK_M = 128
DV_M = 128
W_M = H_M * DV_M
H_F = 8
DH_F = 64
W_F = H_F * DH_F
D_FF = -(-8 * D_MODEL // (3 * 256)) * 256
PLE_DIM = 256
CHUNK = 128
Q_BLOCK = 128
EPS = 1e-6
F_SCALE = DH_F ** -0.5
K_SCALE_M = DK_M ** -0.5
SPLIT_SIZES = (W_M, W_M, W_M, W_M, H_M, H_M, W_F, W_F, W_F, H_F, D_MODEL, D_MODEL)
D_IN = sum(SPLIT_SIZES)

kernel_name = 'mlstm_fox_gated_hybrid_step'

def rmsnorm(x, g):
    xf = x.astype(jnp.float32)
    y = xf * lax.rsqrt(jnp.mean(xf * xf, axis=-1, keepdims=True) + EPS)
    return (y * g.astype(jnp.float32)).astype(x.dtype)

def project_in(x, g_mix, w_in, b_mi, b_mf, b_ff, g_qn, g_kn):
    bn, t = x.shape[:2]
    z = rmsnorm(x, g_mix) @ w_in
    parts = []
    off = 0
    for s in SPLIT_SIZES:
        parts.append(z[..., off:off + s])
        off += s
    mq, mk, mv, mo, mi, mf, fq, fk, fv, ff, ga, gb = parts
    mq = mq.reshape(bn, t, H_M, DK_M)
    mk = mk.reshape(bn, t, H_M, DK_M) * K_SCALE_M
    mv = mv.reshape(bn, t, H_M, DV_M)
    m_ig = (mi + b_mi).astype(jnp.float32)
    m_lf = jax.nn.log_sigmoid((mf + b_mf).astype(jnp.float32))
    fq = rmsnorm(fq.reshape(bn, t, H_F, DH_F), g_qn)
    fk = rmsnorm(fk.reshape(bn, t, H_F, DH_F), g_kn)
    fv = fv.reshape(bn, t, H_F, DH_F)
    f_lf = jax.nn.log_sigmoid((ff + b_ff).astype(jnp.float32))
    return (mq, mk, mv, mo, m_ig, m_lf), (fq, fk, fv, f_lf), (ga, gb)

def mlstm_chunk(carry, xs):
    c_st, n_st, m_st = carry
    q, k, v, ig, lf = xs
    q, k, v = (a.astype(jnp.float32).transpose(0, 2, 1, 3) for a in (q, k, v))
    ig = ig.transpose(0, 2, 1)
    lf = lf.transpose(0, 2, 1)
    length = q.shape[2]
    b = jnp.cumsum(lf, axis=-1)
    a = b + m_st[..., None]
    causal = jnp.tril(jnp.ones((length, length), dtype=bool))
    dlog = jnp.where(causal, b[..., :, None] - b[..., None, :] + ig[..., None, :], -jnp.inf)
    m_t = jnp.maximum(a, jnp.max(dlog, axis=-1))
    w_intra = jnp.exp(dlog - m_t[..., None])
    w_inter = jnp.exp(a - m_t)
    s = jnp.einsum('bhtd,bhsd->bhts', q, k) * w_intra
    num = w_inter[..., None] * jnp.einsum('bhtd,bhde->bhte', q, c_st) + jnp.einsum('bhts,bhse->bhte', s, v)
    den = w_inter * jnp.einsum('bhtd,bhd->bht', q, n_st) + jnp.sum(s, axis=-1)
    h = num / jnp.maximum(jnp.abs(den), jnp.exp(-m_t))[..., None]
    b_end = b[..., -1]
    a_end = b_end + m_st
    w_log = b_end[..., None] - b + ig
    m_new = jnp.maximum(a_end, jnp.max(w_log, axis=-1))
    w_s = jnp.exp(w_log - m_new[..., None])
    decay = jnp.exp(a_end - m_new)
    c_new = decay[..., None, None] * c_st + jnp.einsum('bhs,bhsd,bhse->bhde', w_s, k, v)
    n_new = decay[..., None] * n_st + jnp.einsum('bhs,bhsd->bhd', w_s, k)
    return (c_new, n_new, m_new), h.transpose(0, 2, 1, 3)

def mlstm_prompt(q, k, v, ig, lf):
    bn, s = q.shape[:2]
    nc = s // CHUNK

    def chunks(a):
        return a.reshape((bn, nc, CHUNK) + a.shape[2:]).swapaxes(0, 1)

    init = (jnp.zeros((bn, H_M, DK_M, DV_M), jnp.float32),
            jnp.zeros((bn, H_M, DK_M), jnp.float32),
            jnp.zeros((bn, H_M), jnp.float32))
    (c_f, n_f, m_f), h = lax.scan(mlstm_chunk, init, (chunks(q), chunks(k), chunks(v), chunks(ig), chunks(lf)))
    h = h.swapaxes(0, 1).reshape(bn, s, H_M, DV_M)
    return h, c_f, n_f, m_f

def fox_prompt(q, k, v, lf):
    bn, s = q.shape[:2]
    nb = s // Q_BLOCK
    f_cum = jnp.cumsum(lf, axis=1)
    f_keys = f_cum.transpose(0, 2, 1)
    kpos = jnp.arange(s)

    def block(args):
        qb, fb, start = args
        logits = jnp.einsum('bthd,bshd->bhts', qb, k).astype(jnp.float32) * F_SCALE
        logits = logits + fb.transpose(0, 2, 1)[..., None] - f_keys[:, :, None, :]
        qpos = start + jnp.arange(Q_BLOCK)
        logits = jnp.where(kpos[None, :] <= qpos[:, None], logits, -jnp.inf)
        p = jax.nn.softmax(logits, axis=-1)
        return jnp.einsum('bhts,bshd->bthd', p.astype(v.dtype), v)

    qs = q.reshape(bn, nb, Q_BLOCK, H_F, DH_F).swapaxes(0, 1)
    fs = f_cum.reshape(bn, nb, Q_BLOCK, H_F).swapaxes(0, 1)
    starts = jnp.arange(nb) * Q_BLOCK
    out = lax.map(block, (qs, fs, starts))
    return out.swapaxes(0, 1).reshape(bn, s, H_F, DH_F)

def fox_sample(q, k, v, lf, cache_k, cache_v, cache_lf, page_table):
    db, t = q.shape[:2]
    kp = cache_k[page_table].reshape(db, -1, H_F, DH_F)
    vp = cache_v[page_table].reshape(db, -1, H_F, DH_F)
    lfp = cache_lf[page_table].reshape(db, -1, H_F).astype(jnp.float32)
    n_past = kp.shape[1]
    past_cum = jnp.cumsum(lfp, axis=1)
    f_past = (past_cum - past_cum[:, -1:]).transpose(0, 2, 1)
    f_new = jnp.cumsum(lf, axis=1).transpose(0, 2, 1)
    lp = jnp.einsum('bthd,bshd->bhts', q, kp).astype(jnp.float32) * F_SCALE
    lp = lp + f_new[..., None] - f_past[:, :, None, :]
    ln = jnp.einsum('bthd,bshd->bhts', q, k).astype(jnp.float32) * F_SCALE
    ln = ln + f_new[..., None] - f_new[:, :, None, :]
    ln = jnp.where(jnp.tril(jnp.ones((t, t), dtype=bool)), ln, -jnp.inf)
    p = jax.nn.softmax(jnp.concatenate([lp, ln], axis=-1), axis=-1).astype(v.dtype)
    return (jnp.einsum('bhts,bshd->bthd', p[..., :n_past], vp)
            + jnp.einsum('bhts,bshd->bthd', p[..., n_past:], v))

def merge_out(x, y_m, m_o, g_mh, y_f, gates, w_pa, w_pb, w_out):
    bn, t = x.shape[:2]
    hm = rmsnorm(y_m.astype(x.dtype), g_mh) * jax.nn.sigmoid(m_o).reshape(bn, t, H_M, DV_M)
    a = hm.reshape(bn, t, W_M) @ w_pa
    b = y_f.reshape(bn, t, W_F) @ w_pb
    ga, gb = gates
    return x + (jax.nn.sigmoid(ga) * a + jax.nn.sigmoid(gb) * b) @ w_out

def ffn_and_ple(x, p, g_ffn, w_gu, w_down, g_ple, w_ple_gate, w_ple_proj):
    gu = rmsnorm(x, g_ffn) @ w_gu
    x = x + (jax.nn.silu(gu[..., :D_FF]) * gu[..., D_FF:]) @ w_down
    gate = jax.nn.sigmoid(rmsnorm(x, g_ple) @ w_ple_gate)
    return x + gate * (p.astype(x.dtype) @ w_ple_proj)

def setup_inputs(seed: int = 0) -> dict:
    key = jax.random.key(seed)
    ks = iter(jax.random.split(key, 48))
    f32 = jnp.float32

    def nrm(shape, scale):
        return jax.random.normal(next(ks), shape, f32) * scale

    n_pages = PAST_LEN // PAGE_SIZE
    n_used = DEC_BATCH * n_pages
    n_pool = n_used + n_used // 4
    page_table = jax.random.permutation(next(ks), n_pool)[:n_used].reshape(DEC_BATCH, n_pages).astype(jnp.int32)
    return {
        'x_prompt': nrm((BATCH, SEQ, D_MODEL), 1.0),
        'x_sample': nrm((DEC_BATCH, DEC_SEQ, D_MODEL), 1.0),
        'p_prompt': nrm((DEPTH, BATCH, SEQ, PLE_DIM), 1.0),
        'p_sample': nrm((DEPTH, DEC_BATCH, DEC_SEQ, PLE_DIM), 1.0),
        'cache_k': nrm((DEPTH, n_pool, PAGE_SIZE, H_F, DH_F), 1.0),
        'cache_v': nrm((DEPTH, n_pool, PAGE_SIZE, H_F, DH_F), 1.0),
        'cache_logf': jax.nn.log_sigmoid(2.5 + nrm((DEPTH, n_pool, PAGE_SIZE, H_F), 1.0)),
        'state_C': nrm((DEPTH, DEC_BATCH, H_M, DK_M, DV_M), 0.1),
        'state_n': nrm((DEPTH, DEC_BATCH, H_M, DK_M), 0.1),
        'state_m': nrm((DEPTH, DEC_BATCH, H_M), 1.0),
        'page_table': page_table,
        'g_mix': 1.0 + nrm((DEPTH, D_MODEL), 0.02),
        'w_in': nrm((DEPTH, D_MODEL, D_IN), D_MODEL ** -0.5),
        'b_mi': nrm((DEPTH, H_M), 0.1),
        'b_mf': jnp.linspace(3.0, 6.0, H_M, dtype=f32)[None, :] + nrm((DEPTH, H_M), 0.1),
        'b_ff': jnp.linspace(1.0, 4.0, H_F, dtype=f32)[None, :] + nrm((DEPTH, H_F), 0.1),
        'g_mh': 1.0 + nrm((DEPTH, H_M, DV_M), 0.02),
        'g_qn': 1.0 + nrm((DEPTH, DH_F), 0.02),
        'g_kn': 1.0 + nrm((DEPTH, DH_F), 0.02),
        'w_pa': nrm((DEPTH, W_M, D_MODEL), W_M ** -0.5),
        'w_pb': nrm((DEPTH, W_F, D_MODEL), W_F ** -0.5),
        'w_out': nrm((DEPTH, D_MODEL, D_MODEL), D_MODEL ** -0.5),
        'g_ffn': 1.0 + nrm((DEPTH, D_MODEL), 0.02),
        'w_gu': nrm((DEPTH, D_MODEL, 2 * D_FF), D_MODEL ** -0.5),
        'w_down': nrm((DEPTH, D_FF, D_MODEL), D_FF ** -0.5),
        'g_ple': 1.0 + nrm((DEPTH, D_MODEL), 0.02),
        'w_ple_gate': nrm((DEPTH, D_MODEL, D_MODEL), D_MODEL ** -0.5),
        'w_ple_proj': nrm((DEPTH, PLE_DIM, D_MODEL), PLE_DIM ** -0.5),
    }

def reference(x_prompt, x_sample, p_prompt, p_sample, cache_k, cache_v, cache_logf, state_C, state_n, state_m,
              page_table, g_mix, w_in, b_mi, b_mf, b_ff, g_mh, g_qn, g_kn, w_pa, w_pb, w_out, g_ffn, w_gu,
              w_down, g_ple, w_ple_gate, w_ple_proj):
    xp = x_prompt
    xs = x_sample
    kp_l, vp_l, lfp_l, cp_l, np_l, mp_l = [], [], [], [], [], []
    ks_l, vs_l, lfs_l, cs_l, ns_l, ms_l = [], [], [], [], [], []
    for l in range(DEPTH):
        mi, fi, gates = project_in(xp, g_mix[l], w_in[l], b_mi[l], b_mf[l], b_ff[l], g_qn[l], g_kn[l])
        mq, mk, mv, mo, mig, mlf = mi
        fq, fk, fv, flf = fi
        hm, c_f, n_f, m_f = mlstm_prompt(mq, mk, mv, mig, mlf)
        yf = fox_prompt(fq, fk, fv, flf)
        xp = merge_out(xp, hm, mo, g_mh[l], yf, gates, w_pa[l], w_pb[l], w_out[l])
        xp = ffn_and_ple(xp, p_prompt[l], g_ffn[l], w_gu[l], w_down[l], g_ple[l], w_ple_gate[l], w_ple_proj[l])
        kp_l.append(fk); vp_l.append(fv); lfp_l.append(flf)
        cp_l.append(c_f); np_l.append(n_f); mp_l.append(m_f)

        mi, fi, gates = project_in(xs, g_mix[l], w_in[l], b_mi[l], b_mf[l], b_ff[l], g_qn[l], g_kn[l])
        mq, mk, mv, mo, mig, mlf = mi
        fq, fk, fv, flf = fi
        carry = (state_C[l].astype(jnp.float32), state_n[l].astype(jnp.float32), state_m[l].astype(jnp.float32))
        (c_s, n_s, m_s), hm = mlstm_chunk(carry, (mq, mk, mv, mig, mlf))
        yf = fox_sample(fq, fk, fv, flf, cache_k[l], cache_v[l], cache_logf[l], page_table)
        xs = merge_out(xs, hm, mo, g_mh[l], yf, gates, w_pa[l], w_pb[l], w_out[l])
        xs = ffn_and_ple(xs, p_sample[l], g_ffn[l], w_gu[l], w_down[l], g_ple[l], w_ple_gate[l], w_ple_proj[l])
        ks_l.append(fk); vs_l.append(fv); lfs_l.append(flf)
        cs_l.append(c_s); ns_l.append(n_s); ms_l.append(m_s)

    return (xp, xs,
            jnp.stack(kp_l), jnp.stack(vp_l), jnp.stack(lfp_l),
            jnp.stack(cp_l), jnp.stack(np_l), jnp.stack(mp_l),
            jnp.stack(ks_l), jnp.stack(vs_l), jnp.stack(lfs_l),
            jnp.stack(cs_l), jnp.stack(ns_l), jnp.stack(ms_l))


_drawn_inputs = setup_inputs


def setup_inputs(seed=0):
    import zlib

    import numpy as np

    out = dict(_drawn_inputs(seed))
    spreads = {}
    factors = {'g_mh': 8.0, 'g_qn': 8.0, 'g_kn': 2.798, 'g_ffn': 4.319, 'g_ple': 8.0}
    for name, (base, spread) in spreads.items():
        noise = np.random.default_rng([zlib.crc32(name.encode()), seed]).standard_normal(out[name].shape)
        drawn = base * np.exp(spread * noise) if base else spread * noise
        out[name] = jnp.asarray(drawn.astype(out[name].dtype))
    for name, factor in factors.items():
        out[name] = (out[name] * factor).astype(out[name].dtype)
    return out
```

```python
from contextlib import ExitStack

import concourse.bass as bass
from concourse import mybir

F32 = mybir.dt.float32
F32R = mybir.dt.float32r
BF16 = mybir.dt.bfloat16
I32 = mybir.dt.int32
ALU = mybir.AluOpType
ACT = mybir.ActivationFunctionType
AX = mybir.AxisListType

P = 128
D = 1024
KC = D // P
SEQ = 1024
DB, DS = 8, 4
NS = DB * DS
T = SEQ + NS
NT = 3
TW = T // NT
HM, DM = 4, 128
HF, DH = 8, 64
W = 512
NCH = SEQ // P
PAGES, PAGE = 4, 128
NFF = 22
FF = NFF * P
PLE = 256
EPS = 1e-6
NEG = -1e30
NPOOL = 40
GB = 4
OFF_MI, OFF_FQ, OFF_FF, OFF_MO, OFF_GA = 2048, 2056, 3592, 1536, 3600
GW = 96
KB = 1024


def program(nc, a, o):
    ctx = ExitStack()
    with ctx:
        def at(name, kb, shape, dt=F32):
            return nc.alloc_sbuf_tensor_at(name, shape, dt, offset=BASE + kb)

        made = []

        def sem(name):
            made.append(ctx.enter_context(nc.semaphore(name)))
            return made[-1]

        BASE = 16512
        ROOM = 212800
        b01 = [ctx.enter_context(nc.psum_tensor(f"bank{i}", [P, 512], F32)) for i in range(2)]
        PAIR = [ctx.enter_context(nc.psum_tensor(f"pair{i}", [P, 1024], F32)) for i in range(3)]
        BANK = b01 + [PAIR[i][:, j * 512:(j + 1) * 512] for i in range(3) for j in range(2)]

        top = [0]

        def take(name, shape, dt=F32):
            n = 1
            for s in shape[1:]:
                n *= s
            size = (n * (2 if dt == BF16 else 4) + 31) // 32 * 32
            t = at(name, top[0], shape, dt)
            top[0] += size
            return t

        ident = take("ident", [P, P])
        ones = take("ones", [P, P])
        epsc = take("epsc", [P, 1])
        attn_consts = top[0]
        identb = take("identb", [P, P], BF16)
        maskb = take("maskb", [P, P], BF16)
        maskT = take("maskT", [P, P])
        maskS = take("maskS", [NS, NS])
        col = take("col", [P, NCH + 1, GW])
        gqk = take("gqk", [P, 2, DH])
        attn_consts_end = top[0]
        acth = take("acth", [P, KC, T], F32R)
        actl = take("actl", [P, KC, T], F32R)
        phase_base = top[0]

        xt = take("xt", [P, 2, D])
        xn = take("xn", [P, 2, D])
        gmix = take("gmix", [P, D])
        ssq = take("ssq", [P, 4])
        wg = take("wg", [P, KC, GW])
        wgh = take("wgh", [P, KC, GW], F32R)
        wgl = take("wgl", [P, KC, GW], F32R)
        p1_small = top[0]
        top[0] = phase_base
        gx = take("gx", [GW, T])
        gt = take("gt", [GW, T])
        glf = take("glf", [GW, T])
        rr = take("rr", [GW, T])
        keep = take("keep", [HM, T])
        mlf = take("mlf", [HM, T])
        lfm = take("lfm", [HM, T])
        igm = take("igm", [HM, T])
        m_row = take("m_row", [HM, T])
        ms_row = take("ms_row", [HM, T])
        b_row = gt[0:HM, :]
        top[0] = max(top[0], p1_small)
        wraw = take("wraw", [P, 4, 2, W])
        wh1 = take("wh1", [P, 2, KC, W], F32R)
        wl1 = take("wl1", [P, 2, KC, W], F32R)
        stage = take("stage", [P, 3, W])
        gbias = take("gbias", [GW, 1])
        sm = take("sm", [HM, DB])
        smt = take("smt", [HM, DB])
        assert top[0] <= ROOM, top[0]

        top[0] = phase_base
        fraw = take("fraw", [P, 3, KC, P])
        fwh = take("fwh", [P, 3, KC, P], F32R)
        fwl = take("fwl", [P, 3, KC, P], F32R)
        fout = take("fout", [P, 3, T])
        attn_base = top[0]
        q_in = take("q_in", [P, NCH + 1, DM])
        k_in = take("k_in", [P, NCH + 1, DM])
        v_in = take("v_in", [P, NCH + 1, DM])
        rB = take("rB", [P, T])
        aB = take("aB", [P, T])
        nmB = take("nmB", [P, T])
        cst = take("cst", [P, DB, DM])
        cnew = take("cnew", [P, DB, DM])
        gcur = take("gcur", [P, NCH + 1])
        ncur = take("ncur", [P, DB])
        nnew = take("nnew", [P, DB])
        nst = take("nst", [P, DB * HM])
        nst_in = take("nst_in", [DB * HM, P])
        qT = take("qT", [P, T])
        kT = take("kT", [P, T])
        qs = take("qs", [P, T])
        sw = take("sw", [P, T])
        kw = take("kw", [P, NCH, DM])
        kws = take("kws", [NS, DB, DM])
        states = take("states", [P, NCH, DM])
        nstates = take("nstates", [P, NCH])
        dd = take("dd", [P, T])
        hb = take("hb", [P, T])
        nout = take("nout", [P, HM * (DB + 1)])
        nrow = take("nrow", [HM * (DB + 1), P])
        assert top[0] <= ROOM, top[0]
        pA = PAIR[0]
        pB = PAIR[1]
        pS, pN = BANK[6], BANK[7]

        top[0] = phase_base + KC * P * 4
        qn = take("qn", [P, NCH, 2, DH])
        kn = take("kn", [P, NCH, 2, DH])
        top[0] = attn_base
        q3 = take("q3", [P, NCH, DH])
        k3 = take("k3", [P, NCH, DH])
        v3 = take("v3", [P, NCH, DH])
        nF = take("nF", [P, SEQ])
        qst = take("qst", [P, SEQ], F32R)
        khh = take("khh", [P, SEQ], F32R)
        klo = take("klo", [DH, SEQ], F32R)
        lg = take("lg", [P, 2, SEQ])
        pth = take("pth", [P, 20 * 256], F32R)
        ptl = take("ptl", [P, 20 * 256], F32R)
        vh = take("vh", [P, NCH, P], F32R)
        vl = take("vl", [P, NCH, P], F32R)
        yb = take("yb", [DH, SEQ])
        ss = take("ss", [P, 3, 2 * NCH])
        mx = take("mx", [P, NCH])
        fcol = take("fcol", [P, NCH])
        waits = take("waits", [P, 1])
        nb = take("nb", [P, NCH])
        assert top[0] <= ROOM, top[0]
        pC = PAIR[2]

        XR = at("XR", ROOM - KC * T * 4, [P, KC, T])

        top[0] = phase_base
        kpg = take("kpg", [P, GB, PAGES, W])
        vpg = take("vpg", [P, GB, PAGES, W])
        ktp = take("ktp", [P, 4, PAGES * PAGE])
        lfp = take("lfp", [P, DB * PAGES, HF])
        lfr = take("lfr", [P, GB * PAGES, HF, DS])
        sufm = take("sufm", [P, PAGES * PAGE])
        mc01 = take("mc01", [NS, NS])
        nmc = take("nmc", [NS, NS])
        maskq = take("maskq", [NS, NS])
        qk4 = take("qk4", [NS, 2, HF, DH])
        sq4b = take("sq4b", [NS, 2, HF, DH])
        v4 = take("v4", [NS, W])
        ss4 = take("ss4", [NS, 3, 2 * HF])
        qT4 = take("qT4", [P, 4, NS])
        kT4 = take("kT4", [P, 4, NS])
        qz = take("qz", [P, 4, GB, HF, DS])
        sel = take("sel", [NS, GB, HF, DS])
        lfq = take("lfq", [NS, GB, HF, DS])
        lf4 = take("lf4", [NS, HF, DS])
        px = take("px", [P, PAGES * PAGE + NS])
        pT4 = take("pT4", [P, PAGES + 1, P])
        mx4 = take("mx4", [P, 4])
        ysg = take("ysg", [P, 4, GB, DS])
        ptb = take("ptb", [1, DB * PAGES], I32)
        assert top[0] <= ROOM - KC * T * 4, top[0]
        xr4 = at("xr4", phase_base + GB * PAGES * W * 4, [P, NCH, D])
        xs4 = at("xs4", phase_base + 2 * GB * PAGES * W * 4, [NS, D])

        top[0] = phase_base
        raw = take("raw", [P, 2, D])
        wha = take("wha", [P, 2, D], F32R)
        wla = take("wla", [P, 2, D], F32R)
        t_base = top[0]
        th = take("th", [P, KC, T], F32R)
        tl = take("tl", [P, KC, T], F32R)
        t_end = top[0]
        top[0] = t_base
        rvm = take("rvm", [P, HM, T])
        mo5 = take("mo5", [P, HM, T])
        assert top[0] == t_base + KC * T * 4
        tpart = take("tpart", [P, KC, T])
        top[0] = t_base + KC * T * 4
        yst5 = take("yst5", [P, HM, T])
        hst5 = take("hst5", [P, HM, T])
        top[0] = t_base
        whb = take("whb", [P, 4, D], F32R)
        wlb = take("wlb", [P, 4, D], F32R)
        h_base = top[0]
        hh = take("hh", [P, 2, T], F32R)
        hl = take("hl", [P, 2, T], F32R)
        pjr = take("pjr", [P, 2, 2, P])
        pjh = take("pjh", [P, 2, 2, P], F32R)
        pjl = take("pjl", [P, 2, 2, P], F32R)
        yst7 = take("yst7", [P, 2, NCH + 1, P])
        assert top[0] <= t_end
        top[0] = t_base
        pTh = take("pTh", [P, 2, T], F32R)
        pTl = take("pTl", [P, 2, T], F32R)
        pin = take("pin", [P, NCH + 1, PLE])
        assert top[0] <= h_base
        top[0] = h_base
        yq = take("yq", [P, 2, T])
        top[0] = t_end
        gs = take("gs", [P, 2, T])
        assert top[0] <= ROOM - KC * T * 4, top[0]
        top[0] = attn_consts
        tmp = take("tmp", [P, NT, TW])
        gv = take("gv", [P, HM + 2 * KC])
        gc = take("gc", [P, 2])
        assert top[0] <= attn_consts_end, top[0]
        top[0] = t_end
        rv = take("rv", [P, NT, TW])
        gn = take("gn", [P, 2, TW])
        assert top[0] <= t_end + 2 * T * 4
        top[0] = attn_consts
        un = take("un", [P, 2, TW])
        sqt = tmp

        def lg_bank(i):
            at = i % 2 * 512 if i < 4 else 0
            return pA[:, at:at + (i + 1) * P]

        def tp_bank(i):
            at = i % 2 * 512 if i < 4 else 0
            return pB[:, at:at + (i + 1) * P].rearrange("p (j t) -> p j t", t=P)

        def pt_view(x, i):
            m = i // 2
            base = m * (m + 1) * 256
            return x[:, base:base + (2 * m + 2) * 256].rearrange("p (j t) -> p j t", t=256)[:, 0:i + 1, i % 2 * P:(i % 2 + 1) * P]

        def colF(i):
            return fcol[:, i:i + 1]

        def kt_bank(s):
            return (pA, pB)[s % 4 // 2][:, s % 2 * 512:(s % 2 + 1) * 512]

        class Chain:

            def __init__(self, eng, s):
                self.eng, self.sem, self.base, self.k, self.g, self.per = eng, s, 0, 0, 0, 0

            def enter(self, g, per):
                self.g, self.per, self.base, self.k = g, per, self.base + self.k, 0

            def leave(self, turns):
                assert self.k == self.per, (self.k, self.per)
                self.base, self.k, self.g, self.per = self.base + turns * self.per, 0, 0, 0

            def step(self, ins):
                ins.then_inc(self.sem, 1)
                self.k += 1
                self.eng.wait_ge(self.sem, self.base + self.k + (self.g * self.per if self.per else 0))

        phase_done = sem("phase_done")

        def end_phase(eng):
            eng.drain().then_inc(phase_done, 1)

        def begin_phase(eng, n):
            eng.wait_ge(phase_done, 5 * (n - 1))

        consts = sem("consts")
        x_in = [sem("x_in0"), sem("x_in1")]
        small_in = sem("small_in")
        ssum_done = sem("ssum_done")
        sq_done = sem("sq_done")
        xn_done = sem("xn_done")
        xt_done = sem("xt_done")
        xhi_done = sem("xhi_done")
        xlo_done = sem("xlo_done")
        dve_own = sem("dve_own")
        act_own = sem("act_own")
        pool_own = sem("pool_own")
        pool_own2 = sem("pool_own2")
        wg_in = sem("wg_in")
        wg_hi = sem("wg_hi")
        wg_lo = sem("wg_lo")
        gate_mm = sem("gate_mm")
        gate_x = sem("gate_x")
        gate_l = sem("gate_l")
        rows_done = sem("rows_done")
        rows_out = sem("rows_out")
        col_mm = sem("col_mm")
        col_done = sem("col_done")
        w_in1 = [sem(f"w_in1_{i}") for i in range(4)]
        w_hi1 = sem("w_hi1")
        w_lo1 = sem("w_lo1")
        unit_mm = sem("unit_mm")
        unit_out = sem("unit_out")
        unit_st = [sem(f"unit_st{i}") for i in range(3)]
        misc_out = sem("misc_out")

        nst_ld = sem("nst_ld")
        nst_t = sem("nst_t")
        fw_in = [sem(f"fw_in{i}") for i in range(3)]
        f_hi = sem("f_hi")
        f_lo = sem("f_lo")
        f_mm = sem("f_mm")
        f_out = sem("f_out")
        f_st = [sem(f"f_st{i}") for i in range(3)]
        qkv_in = sem("qkv_in")
        rows_in = sem("rows_in")
        cs_in = sem("cs_in")
        gcur_done = sem("gcur_done")
        rm_done = sem("rm_done")
        wint_done = sem("wint_done")
        e_done = sem("e_done")
        tq_mm = sem("tq_mm")
        qkt_done = sem("qkt_done")
        qs_done = sem("qs_done")
        kw_done = sem("kw_done")
        s_mm = sem("s_mm")
        sw_done = sem("sw_done")
        u_mm = sem("u_mm")
        c_done = sem("c_done")
        den_mm = sem("den_mm")
        abs_done = sem("abs_done")
        h_done = sem("h_done")
        us_mm = sem("us_mm")
        head_done = sem("head_done")
        h_st = sem("h_st")
        n_mm = sem("n_mm")
        n_done = sem("n_done")

        g_in = sem("g_in")
        g_done = sem("g_done")
        qkv3_in = sem("qkv3_in")
        nF_in = sem("nF_in")
        sq3 = sem("sq3")
        ms3 = sem("ms3")
        rs3 = sem("rs3")
        ri3 = sem("ri3")
        norm3 = sem("norm3")
        k_st = sem("k_st")
        v_hi = sem("v_hi")
        v_lo = sem("v_lo")
        tqk_mm = sem("tqk_mm")
        qk_hi = sem("qk_hi")
        qk_lo = sem("qk_lo")
        lg_mm = sem("lg_mm")
        nb_done = sem("nb_done")
        p_done = sem("p_done")
        tp_mm = sem("tp_mm")
        pt_hi = sem("pt_hi")
        pt_lo = sem("pt_lo")
        pv_mm = sem("pv_mm")
        y_done = sem("y_done")
        y_st = sem("y_st")

        s4_in = sem("s4_in")
        pt_in = sem("pt_in")
        kpg_in = [sem(f"kpg_in{i}") for i in range(GB)]
        vpg_in = sem("vpg_in")
        lfp_in = [sem("lfp_in0"), sem("lfp_in1")]
        lf_ready = sem("lf_ready")
        sq4 = sem("sq4")
        ms4 = sem("ms4")
        rs4 = sem("rs4")
        qk4_done = sem("qk4_done")
        tq4_mm = sem("tq4_mm")
        k4_st = sem("k4_st")
        grp_done = sem("grp_done")
        kt_mm = sem("kt_mm")
        kt_a = sem("kt_a")
        kt_d = sem("kt_d")
        l4_mm = sem("l4_mm")
        nb4 = sem("nb4")
        e4_done = sem("e4_done")
        p4_done = sem("p4_done")
        tp4_mm = sem("tp4_mm")
        pt4_done = sem("pt4_done")
        o4_mm = sem("o4_mm")
        o4_out = sem("o4_out")
        ot4_mm = sem("ot4_mm")
        y4_done = sem("y4_done")
        y4_st = sem("y4_st")

        x4_in = [sem(f"x4_in{i}") for i in range(3)]
        x4_mm = sem("x4_mm")
        x4_a = sem("x4_a")
        x4_d = sem("x4_d")

        past = [x for x in made if x not in (phase_done, consts, dve_own, act_own, pool_own, pool_own2)]
        reused = []

        def again(name):
            reused.append(past[len(reused)])
            return reused[-1]

        started = sem("started")
        cleared = sem("cleared")
        gv_in = again("gv_in")
        y5_in = [again("y5_in0"), again("y5_in1")]
        h5_in = again("h5_in")
        mo5_in = again("mo5_in")
        g5_in = [again("g5_in0"), again("g5_in1")]
        w_ld = [again("w_ld0"), again("w_ld1")]
        w_split = again("w_split")
        y5_hi = again("y5_hi")
        y5_lo = again("y5_lo")
        mo_sig = again("mo_sig")
        g5_sig = again("g5_sig")
        hsq = again("hsq")
        hss_mm = again("hss_mm")
        hln = again("hln")
        hrv = again("hrv")
        hm_done = again("hm_done")
        hm_hi = again("hm_hi")
        hm_lo = again("hm_lo")
        b_mm = again("b_mm")
        b_done = again("b_done")
        a_mm = again("a_mm")
        t_done = again("t_done")
        t_hi = again("t_hi")
        t_lo = again("t_lo")
        o_mm = again("o_mm")
        gc_done = again("gc_done")
        x5_done = again("x5_done")
        sq5 = again("sq5")
        ss5_mm = again("ss5_mm")
        xg_hi = again("xg_hi")
        xg_lo = again("xg_lo")
        rv_zero = again("rv_zero")
        rv_done = again("rv_done")
        gu_mm = again("gu_mm")
        gn_done = again("gn_done")
        un_done = again("un_done")
        sl_done = again("sl_done")
        hd_done = again("hd_done")
        h_hi = again("h_hi")
        h_lo = again("h_lo")
        dn_mm = again("dn_mm")
        x6_done = again("x6_done")
        p_in = again("p_in")
        pj_ld = [again("pj_ld0"), again("pj_ld1")]
        pj_split = again("pj_split")
        xp_hi = again("xp_hi")
        xp_lo = again("xp_lo")
        sq7 = again("sq7")
        ss7_mm = again("ss7_mm")
        rv7_done = again("rv7_done")
        pt7_mm = again("pt7_mm")
        pt7_hi = again("pt7_hi")
        pt7_lo = again("pt7_lo")
        pg_mm = again("pg_mm")
        pgn = again("pgn")
        sg7 = again("sg7")
        y7_done = again("y7_done")
        yt_mm = again("yt_mm")
        yt_out = again("yt_out")
        y7_st = [again("y7_st0"), again("y7_st1")]
        spare = again("spare")

        XTILES = NCH + 1
        PIECES = 4
        GROUPS = 6
        zA_rows = o["zA"]
        zA_v = zA_rows.rearrange("(q t) n -> q t n", t=T)

        def trows(i):
            return P if i < NCH else NS

        block = ctx.enter_context(nc.Block())

        @block.sync
        def _(sp):
            sp.dma_start(gmix[:], a["g_mix"][0].partition_broadcast(P)).then_inc(small_in, 16)
            sp.wait_ge(consts, 1)
            sp.dma_start(gbias[0:HM, :], a["b_mi"].rearrange("a h -> h a"), allow_slow_non_contiguous=True).then_inc(small_in, 16)
            sp.dma_start(gbias[32:32 + HM, :], a["b_mf"].rearrange("a h -> h a"), allow_slow_non_contiguous=True).then_inc(small_in, 16)
            sp.dma_start(gbias[64:64 + HF, :], a["b_ff"].rearrange("a h -> h a"), allow_slow_non_contiguous=True).then_inc(small_in, 16)
            sp.dma_start(sm[:], a["state_m"][0].rearrange("b h -> h b"), allow_slow_non_contiguous=True).then_inc(small_in, 16)
            w_v = a["w_in"][0].rearrange("(k p) n -> p k n", p=P)
            for c, n, src in ((0, HM, OFF_MI), (32, HM, OFF_MI + HM), (64, HF, OFF_FF)):
                sp.dma_start(wg[:, :, c:c + n], w_v[:, :, src:src + n], allow_slow_non_contiguous=True).then_inc(wg_in, 16)
            with sp.Fori(0, NCH // 2) as g:
                for s in range(2):
                    row = sp.snap(g * 256 + s * P)
                    sp.wait_ge(xn_done, 2 * g + s + 1)
                    sp.dma_start(xt[:, s], a["x_prompt"][0][bass.ds(row, P), :]).then_inc(x_in[s], 16)
            sp.wait_ge(xn_done, NCH + 1)
            sp.dma_start(xt[0:NS, 0], a["x_sample"].rearrange("b s d -> (b s) d")).then_inc(x_in[0], 16)

            def load_group(g, half):
                colv = sp.snap(g * W + (0 if half == 0 else OFF_FQ))
                for j in range(PIECES):
                    sp.wait_ge(w_lo1, (2 * g + half) * PIECES + j + 1)
                    sp.dma_start(wraw[:, j], w_v[:, 2 * j:2 * j + 2, bass.ds(colv, W)]).then_inc(w_in1[j], 16)

            def store_units(g, half):
                for i in range(XTILES):
                    u = half * XTILES + i
                    rows = trows(i)
                    row0 = sp.snap(g * T + half * 3 * T + i * P)
                    sp.wait_ge(unit_out, g * 18 + u + 1 + 3)
                    sp.dma_start(zA_rows[bass.ds(row0, rows), :], stage[0:rows, u % 3]).then_inc(unit_st[u % 3], 16)

            load_group(0, 0)
            with sp.Fori(0, GROUPS // 2 - 1) as g:
                load_group(g, 1)
                store_units(g, 0)
                load_group(g + 1, 0)
                store_units(g, 1)
            load_group(GROUPS // 2 - 1, 1)
            sp.wait_ge(rows_done, 1)
            RS = o["rows"]
            sp.dma_start(RS[0:HM, :], lfm[:]).then_inc(rows_out, 16)
            sp.dma_start(RS[HM:2 * HM, :], igm[:]).then_inc(rows_out, 16)
            sp.dma_start(RS[2 * HM:3 * HM, :], mlf[:]).then_inc(rows_out, 16)
            sp.dma_start(RS[3 * HM:3 * HM + HF, :], gt[64:64 + HF, :]).then_inc(rows_out, 16)
            sp.dma_start(o["m_prompt"][0].rearrange("b h -> h b"), m_row[:, SEQ - 1:SEQ], allow_slow_non_contiguous=True).then_inc(misc_out, 16)
            sp.dma_start(o["m_sample"][0].rearrange("b h -> h b"), m_row[:, SEQ + DS - 1::DS], allow_slow_non_contiguous=True).then_inc(misc_out, 16)
            store_units(GROUPS // 2 - 1, 0)
            store_units(GROUPS // 2 - 1, 1)
            sp.wait_ge(col_done, 1)
            sp.dma_start(o["logf_prompt"][0, 0].rearrange("(c p) h -> p c h", p=P), col[:, 0:NCH, 64:64 + HF], allow_slow_non_contiguous=True).then_inc(misc_out, 16)
            sp.dma_start(o["logf_sample"][0].rearrange("b s h -> (b s) h"), col[0:NS, NCH, 64:64 + HF]).then_inc(misc_out, 16)
            sp.wait_ge(rows_out, 64)
            sp.wait_ge(misc_out, 64)
            for i in range(3):
                sp.wait_ge(unit_st[i], 16 * (1 + GROUPS * XTILES // 3))
            end_phase(sp)

            begin_phase(sp, 2)

            def load_gate_chunks(g):
                for j in range(3):
                    c = sp.snap(OFF_MO + g * P if j == 0 else OFF_GA + g * 2 * P + (j - 1) * P)
                    sp.wait_ge(f_lo, 3 * g + j + 1)
                    sp.dma_start(fraw[:, j], w_v[:, :, bass.ds(c, P)]).then_inc(fw_in[j], 16)

            def load_qkv(g):
                c = sp.snap(g * DM)
                sp.wait_ge(us_mm, g + 1)
                for q, buf in enumerate((q_in, k_in, v_in)):
                    sp.dma_start(buf[0:NS, NCH, :], zA_v[q][SEQ:T, bass.ds(c, DM)]).then_inc(qkv_in, 16)
                    sp.dma_start(buf[:, 0:NCH, :], zA_v[q][0:SEQ, bass.ds(c, DM)].rearrange("(i p) d -> p i d", p=P)).then_inc(qkv_in, 16)

            def load_rows(g):
                rows = [sp.snap(g + r * HM) for r in range(3)]
                h = sp.snap(g + 0)
                sp.wait_ge(head_done, g + 1)
                for r, buf in zip(rows, (rB, aB, nmB)):
                    sp.dma_start(buf[:], o["rows"][bass.ds(r, 1), :].partition_broadcast(P).rearrange("p a t -> p (a t)")).then_inc(rows_in, 16)
                sp.dma_start(cst[:], a["state_C"][0][:, bass.ds(h, 1)].rearrange("b a d e -> d (b a) e")).then_inc(cs_in, 16)

            sp.dma_start(nst_in[:], a["state_n"][0].rearrange("b h d -> (b h) d")).then_inc(nst_ld, 16)
            load_qkv(0)
            load_gate_chunks(0)
            load_rows(0)
            sp.dma_start(o["v_prompt"][0, 0].rearrange("s h d -> s (h d)"), zA_rows[5 * T:5 * T + SEQ, :]).then_inc(misc_out, 16)
            sp.dma_start(o["v_sample"][0].rearrange("b s h d -> (b s) (h d)"), zA_rows[5 * T + SEQ:6 * T, :]).then_inc(misc_out, 16)
            with sp.Fori(0, HM - 1) as g:
                load_gate_chunks(g + 1)
                load_qkv(g + 1)
                load_rows(g + 1)
            sp.wait_ge(us_mm, HM + 1)
            sp.wait_ge(kw_done, HM)
            sp.wait_ge(f_lo, 3 * HM + 3)
            sp.dma_start(gqk[:, 0, :], a["g_qn"][0].partition_broadcast(P)).then_inc(g_in, 16)
            sp.dma_start(gqk[:, 1, :], a["g_kn"][0].partition_broadcast(P)).then_inc(g_in, 16)

            def load_head(g):
                sp.wait_ge(v_lo, g + 1)
                c = sp.snap(g * DH)
                for q, buf in ((5, v3), (3, q3), (4, k3)):
                    sp.dma_start(buf[:], zA_v[q][0:SEQ, bass.ds(c, DH)].rearrange("(i p) d -> p i d", p=P)).then_inc(qkv3_in, 16)

            def load_row(g):
                sp.wait_ge(nb_done, 8 * g + 8)
                r = sp.snap(g + 3 * HM)
                sp.dma_start(nF[:], o["rows"][bass.ds(r, 1), 0:SEQ].partition_broadcast(P).rearrange("p a t -> p (a t)")).then_inc(nF_in, 16)

            def load_gate(g):
                c = sp.snap(OFF_GA + (8 + g) * P)
                sp.wait_ge(f_lo, g + 3 * HM + 3)
                sp.dma_start(fraw[:, 0], w_v[:, :, bass.ds(c, P)]).then_inc(fw_in[0], 16)

            def store_y(g):
                row = sp.snap(g * DH)
                sp.wait_ge(y_done, 2 * g + 2 + 2)
                sp.dma_start(o["yT"][bass.ds(row, DH), 0:SEQ], yb[:]).then_inc(y_st, 16)

            load_head(0)
            load_gate(0)
            load_row(0)
            sp.wait_ge(n_done, 1)
            sp.dma_start(o["n_prompt"][0, 0], nrow[0:HM, :]).then_inc(misc_out, 16)
            sp.dma_start(o["n_sample"][0].rearrange("b h d -> (b h) d"), nrow[HM:, :]).then_inc(misc_out, 16)
            sp.wait_ge(misc_out, 128)
            end_phase(sp)

            begin_phase(sp, 3)
            with sp.Fori(0, HF - 1) as g:
                load_gate(g + 1)
                load_row(g + 1)
                store_y(g)
            store_y(HF - 1)
            end_phase(sp)

            begin_phase(sp, 4)
            sp.dma_start(ptb[:], a["page_table"].rearrange("b n -> (b n)").unsqueeze(0)).then_inc(pt_in, 16)
            for j, q in ((0, 3), (1, 4)):
                sp.dma_start(qk4[:, j].rearrange("t h d -> t (h d)"), zA_v[q][SEQ:T, :]).then_inc(s4_in, 16)
            sp.dma_start(v4[:], zA_v[5][SEQ:T, :]).then_inc(s4_in, 16)
            for i in range(2):
                sp.dma_start(xr4[:, 4 * i:4 * i + 4, :], a["x_prompt"][0][512 * i:512 * i + 512, :].rearrange("(i p) d -> p i d", p=P)).then_inc(x4_in[i], 16)
            sp.dma_start(xs4[:], a["x_sample"].rearrange("b s d -> (b s) d")).then_inc(x4_in[2], 16)
            sp.wait_ge(pt_in, 16)
            with sp.Fori(0, DB // GB) as g:
                pages = []
                for b in range(GB):
                    pages += [sp.value_load(ptb[0:1, bass.ds(g * (GB * PAGES) + b * PAGES + i, 1)], min_val=0, max_val=NPOOL - 1) for i in range(PAGES)]
                    sp.wait_ge(kt_mm, g * 16 + 4 * b + 4)
                    for i in range(PAGES):
                        sp.dma_start(kpg[:, b, i, :], a["cache_k"][0][bass.ds(pages[b * PAGES + i], 1)].rearrange("a p h d -> p (a h d)")).then_inc(kpg_in[b], 16)
                sp.wait_ge(x4_mm, XTILES)
                sp.wait_ge(o4_mm, g + 1)
                for b in range(GB):
                    for i in range(PAGES):
                        sp.dma_start(vpg[:, b, i, :], a["cache_v"][0][bass.ds(pages[b * PAGES + i], 1)].rearrange("a p h d -> p (a h d)")).then_inc(vpg_in, 16)
            end_phase(sp)

            begin_phase(sp, 5)
            sp.wait_ge(cleared, 1)
            sp.sem_inc(started, 1)

            def load_piece(n, j, src, k):
                sp.wait_ge(w_split, n + 1)
                sp.dma_start(raw[:, j].rearrange("p (k n) -> p k n", k=k), src).then_inc(w_ld[j], 16)

            def chunked(name):
                return a[name][0].rearrange("(k p) n -> p k n", p=P)

            def load_gates(slot, row):
                sp.dma_start(gs[:, slot, :], o["zT"][bass.ds(row, P), :] if not isinstance(row, int) else o["zT"][row:row + P, :]).then_inc(g5_in[slot], 16)

            load_piece(0, 0, chunked("w_pb")[:, :, 0:256], 4)
            for i in range(2):
                sp.dma_start(yst5[:, 2 * i:2 * i + 2, :], o["yT"][256 * i:256 * i + 256, :].rearrange("(c p) t -> p c t", p=P)).then_inc(y5_in[i], 16)
            load_piece(1, 1, chunked("w_pb")[:, :, 256:512], 4)
            sp.dma_start(gv[:, 0:HM], a["g_mh"][0].rearrange("h d -> d h"), allow_slow_non_contiguous=True).then_inc(gv_in, 16)
            for j, g_name in enumerate(("g_ffn", "g_ple")):
                sp.dma_start(gv[:, HM + j * KC:HM + (j + 1) * KC], a[g_name][0].rearrange("(k p) -> p k", p=P),
                             allow_slow_non_contiguous=True).then_inc(gv_in, 16)
            load_gates(0, 12 * P)
            load_gates(1, 13 * P)
            sp.dma_start(mo5[:], o["zT"][0:W, :].rearrange("(c p) t -> p c t", p=P)).then_inc(mo5_in, 16)
            sp.dma_start(hst5[:], o["hT"].rearrange("(c p) t -> p c t", p=P)).then_inc(h5_in, 16)
            for c in range(2, KC):
                if c % 2 == 0 and c < 6:
                    n = c // 2 + 1
                    load_piece(n, n % 2, chunked("w_pb")[:, :, n * 256:(n + 1) * 256], 4)
                sp.wait_ge(b_done, 3 * c + 3)
                load_gates(c % 2, (12 + c) * P)
            sp.wait_ge(b_done, 6 + 3 * KC - 3)
            with sp.Fori(0, 2) as g:
                for j in range(2):
                    c = sp.snap(g * 512 + j * 256)
                    load_piece(g * 2 + 4 + j, j, chunked("w_pa")[:, :, bass.ds(c, 256)], 4)
                    for i in range(2):
                        row = sp.snap(g * 512 + (4 + 2 * j + i) * P)
                        sp.wait_ge(b_done, 6 + 3 * KC - 3 + 3 * i)
                        sp.wait_ge(t_done, g * 12 + 6 * j + 3 * i + 3)
                        load_gates(i, row)
            with sp.Fori(0, KC // 2) as g:
                for j in range(2):
                    c = sp.snap(g * 256 + j * P)
                    load_piece(g * 2 + 8 + j, j, chunked("w_out")[:, :, bass.ds(c, P)], KC)

            with sp.Fori(0, NFF // 2) as g:
                for j in range(6):
                    if j < 4:
                        c = sp.snap(g * 256 + (j // 2) * P + (j % 2) * FF)
                        load_piece(g * 6 + 16 + j, j % 2, chunked("w_gu")[:, :, bass.ds(c, P)], KC)
                    else:
                        r = sp.snap(g * 256 + (j - 4) * P)
                        sp.wait_ge(w_split, g * 6 + 16 + j + 1)
                        sp.dma_start(raw[:, j % 2], a["w_down"][0][bass.ds(r, P), :]).then_inc(w_ld[j % 2], 16)

            sp.wait_ge(dn_mm, 24 + 12 * NFF)
            sp.dma_start(pin[:, 0:NCH, :], a["p_prompt"][0, 0].rearrange("(i p) d -> p i d", p=P)).then_inc(p_in, 16)
            sp.dma_start(pin[0:NS, NCH, :], a["p_sample"][0].rearrange("b s d -> (b s) d")).then_inc(p_in, 16)
            with sp.Fori(0, KC // 2) as g:
                for j in range(2):
                    c = sp.snap(g * 256 + j * P)
                    load_piece(g * 2 + 82 + j, j, chunked("w_ple_gate")[:, :, bass.ds(c, P)], KC)
                    sp.wait_ge(pj_split, g * 2 + j + 1)
                    sp.dma_start(pjr[:, j], chunked("w_ple_proj")[:, :, bass.ds(c, P)]).then_inc(pj_ld[j], 16)
            end_phase(sp)

        @block.gpsimd
        def _(pool):
            nc.gpsimd.memset(epsc[:], EPS)
            nc.gpsimd.memset(wg[:], 0.0)
            nc.gpsimd.memset(gbias[:], 0.0).then_inc(consts, 1)
            nc.gpsimd.memset(ones[:], 1.0)
            nc.gpsimd.memset(ident[:], 0.0).then_inc(pool_own, 1)
            nc.gpsimd.memset(identb[:], 0.0).then_inc(pool_own, 1)
            nc.gpsimd.memset(maskb[:], 0.0).then_inc(pool_own, 1)
            nc.gpsimd.memset(maskT[:], 0.0).then_inc(pool_own, 1)
            nc.gpsimd.memset(maskS[:], 0.0).then_inc(pool_own, 1)
            pool.wait_ge(pool_own, 5)
            for m in (ident, identb):
                nc.gpsimd.affine_select(out=m[:], in_=m[:], compare_op=ALU.not_equal, fill=1.0, base=0,
                                        pattern=[[-1, P]], channel_multiplier=1)
            nc.gpsimd.affine_select(out=maskb[:], in_=maskb[:], compare_op=ALU.is_ge, fill=NEG, base=0,
                                    pattern=[[-1, P]], channel_multiplier=1)
            nc.gpsimd.affine_select(out=maskT[:], in_=maskT[:], compare_op=ALU.is_ge, fill=NEG, base=0,
                                    pattern=[[1, P]], channel_multiplier=-1)
            nc.gpsimd.affine_select(out=maskS[:], in_=maskS[:], compare_op=ALU.is_ge, fill=NEG, base=0,
                                    pattern=[[1, NS]], channel_multiplier=-1).then_inc(pool_own, 1)
            pool.wait_ge(pool_own, 6)
            nc.gpsimd.affine_select(out=maskS[:], in_=maskS[:], compare_op=ALU.is_ge, fill=NEG, base=0,
                                    pattern=[[-DS, DB], [0, DS]], channel_multiplier=1).then_inc(consts, 1)
            pool.wait_ge(wg_hi, 1)
            nc.gpsimd.tensor_tensor(wgl[:], wg[:], wgh[:].bitcast(F32), ALU.subtract).then_inc(wg_lo, 1)
            with pool.Fori(0, GROUPS // 2) as g:
                for half in range(2):
                    for j in range(PIECES):
                        pool.wait_ge(w_hi1, g * 2 * PIECES + half * PIECES + j + 1)
                        nc.gpsimd.tensor_tensor(wl1[:, half, 2 * j:2 * j + 2, :], wraw[:, j],
                                                wh1[:, half, 2 * j:2 * j + 2, :].bitcast(F32),
                                                ALU.subtract).then_inc(w_lo1, 1)
            end_phase(pool)

            begin_phase(pool, 2)

            def split_gate(g, j, per, past=0):
                pool.wait_ge(f_hi, per * g + 3 * past + j + 1)
                nc.gpsimd.tensor_tensor(fwl[:, j], fraw[:, j], fwh[:, j].bitcast(F32), ALU.subtract).then_inc(f_lo, 1)

            def pool_mlstm(g, last):
                rB8 = rB[:, 0:SEQ].rearrange("p (c t) -> p c t", t=P)
                pool.wait_ge(rows_in, 48 * g + 48)
                nc.gpsimd.tensor_tensor(rB8, rB8, maskT[:].unsqueeze(1).to_broadcast([P, NCH, P]), ALU.add).then_inc(pool_own, 1)
                pool.wait_ge(pool_own, 6 + g + 1)
                nc.gpsimd.tensor_tensor(rB[0:NS, SEQ:], rB[0:NS, SEQ:], maskS[:], ALU.add)
                pool.wait_ge(gcur_done, g + 1)
                nc.gpsimd.tensor_tensor(rB8, rB8, gcur[:, 0:NCH].unsqueeze(2).to_broadcast([P, NCH, P]), ALU.add).then_inc(rm_done, 1)
                split_gate(g, 1, 3)
                split_gate(g, 2, 3)
                if not last:
                    split_gate(g + 1, 0, 3)

            split_gate(0, 0, 3)
            with pool.Fori(0, HM - 1) as g:
                pool_mlstm(g, False)
            pool_mlstm(HM - 1, True)
            end_phase(pool)

            begin_phase(pool, 3)
            nc.gpsimd.memset(vh[:, :, DH:].bitcast(F32), 1.0)
            nc.gpsimd.memset(vl[:, :, DH:].bitcast(F32), 0.0).then_inc(consts, 1)

            def norm_head(g):
                pool.wait_ge(ri3, g + 1)
                for j, (x, y) in enumerate(((q3, qn), (k3, kn))):
                    nc.gpsimd.tensor_tensor(x[:], x[:], ss[:, 1, j * NCH:(j + 1) * NCH].unsqueeze(2).to_broadcast([P, NCH, DH]),
                                            ALU.mult).then_inc(pool_own, 1)
                pool.wait_ge(pool_own, 2 * g + 2 + 6 + HM)
                for j, (x, y) in enumerate(((q3, qn), (k3, kn))):
                    for c in range(2):
                        ins = nc.gpsimd.tensor_tensor(y[:, :, c, :], x[:], gqk[:, j:j + 1, :].to_broadcast([P, NCH, DH]), ALU.mult)
                ins.then_inc(norm3, 1)

            def low_values(g):
                pool.wait_ge(v_hi, g + 1)
                nc.gpsimd.tensor_tensor(vl[:, :, 0:DH], v3[:], vh[:, :, 0:DH].bitcast(F32), ALU.subtract).then_inc(v_lo, 1)

            def pool_head(g, last):
                low_values(g)
                if not last:
                    norm_head(g + 1)
                    split_gate(g + 1, 0, 1, HM)

            pool.wait_ge(g_done, 1)
            norm_head(0)
            split_gate(0, 0, 1, HM)
            with pool.Fori(0, HF - 1) as g:
                pool_head(g, False)
            pool_head(HF - 1, True)
            end_phase(pool)

            begin_phase(pool, 4)
            nc.gpsimd.memset(sufm[:], 1.0)
            nc.gpsimd.memset(maskq[:], 0.0).then_inc(pool_own, 1)
            pool.wait_ge(pool_own, 1 + 6 + HM + 2 * HF)
            nc.gpsimd.affine_select(out=sufm[:, (PAGES - 1) * PAGE:], in_=sufm[:, (PAGES - 1) * PAGE:], compare_op=ALU.is_gt, fill=0.0,
                                    base=0, pattern=[[-1, PAGE]], channel_multiplier=1)
            nc.gpsimd.affine_select(out=maskq[:], in_=maskq[:], compare_op=ALU.is_ge, fill=NEG, base=0,
                                    pattern=[[-1, NS]], channel_multiplier=1).then_inc(pool_own, 1)
            pool.wait_ge(pool_own, 2 + 6 + HM + 2 * HF)
            nc.gpsimd.affine_select(out=maskq[:], in_=maskq[:], compare_op=ALU.is_ge, fill=NEG, base=DS - 1,
                                    pattern=[[DS, DB], [0, DS]], channel_multiplier=-1).then_inc(consts, 1)
            pool.wait_ge(pt_in, 16)
            for i in range(DB * PAGES):
                page = pool.value_load(ptb[0:1, i:i + 1], min_val=0, max_val=NPOOL - 1)
                pool.dma_start(lfp[:, i, :], a["cache_logf"][0][bass.ds(page, 1)].rearrange("a p h -> p (a h)")).then_inc(lfp_in[i // (GB * PAGES)], 16)
            for i in range(2):
                pool.wait_ge(lfp_in[i], 16 * GB * PAGES)
                pool.sem_inc(lf_ready, 1)
            end_phase(pool)

            begin_phase(pool, 5)
            pool.wait_ge(cleared, 1)
            pool.sem_inc(started, 1)
            before = 8 + HM + 2 * HF

            def split_piece(n, count, j, hi, lo):
                pool.wait_ge(w_ld[j], count * 16)
                pool.sem_inc(spare, 1)
                nc.gpsimd.tensor_copy(hi, raw[:, j]).then_inc(pool_own, 1)
                pool.wait_ge(pool_own, n + 1 + before)
                nc.gpsimd.tensor_tensor(lo, raw[:, j], hi.bitcast(F32), ALU.subtract).then_inc(w_split, 1)

            for n in range(4):
                if n >= 2:
                    pool.wait_ge(b_mm, 6 * (n - 1))
                split_piece(n, n // 2 + 1, n % 2, wha[:, n % 2], wla[:, n % 2])
            with pool.Fori(0, 2) as g:
                for j in range(2):
                    pool.wait_ge(b_mm, 18 + 6 * j)
                    pool.wait_ge(a_mm, g * 12 + 6 * j + 6)
                    split_piece(g * 2 + 4 + j, g + 3, j, wha[:, j], wla[:, j])
            with pool.Fori(0, KC // 2) as g:
                for j in range(2):
                    pool.wait_ge(a_mm, 12 + 18 + 6 * j)
                    pool.wait_ge(o_mm, g * 6 + 3 * j + 3)
                    split_piece(g * 2 + 8 + j, g + 5, j, wha[:, j], wla[:, j])
            pool.wait_ge(o_mm, 6 + 3 * KC)
            with pool.Fori(0, NFF // 2) as g:
                for j in range(6):
                    if j < 4:
                        pool.wait_ge(gu_mm, g * 6 + 3 * (j // 2) + 3)
                    else:
                        pool.wait_ge(dn_mm, g * 24 + 24)
                    hi, lo = (wha[:, j], wla[:, j]) if j < 2 else (whb[:, j - 2], wlb[:, j - 2])
                    split_piece(g * 6 + 16 + j, g * 3 + 9 + j // 2, j % 2, hi, lo)

            pool.wait_ge(x6_done, 4 + 12 * NFF)
            for n in range(NT * KC):
                t, c = n // KC, n % KC
                x = XR[:, c, t * TW:(t + 1) * TW]
                pool.wait_ge(ss7_mm, n + 1)
                nc.gpsimd.tensor_tensor(sqt[:, n % 3, :], x, x, ALU.mult).then_inc(sq7, 1)
            with pool.Fori(0, KC // 2) as g:
                for j in range(2):
                    pool.wait_ge(gu_mm, 6 + 3 * NFF)
                    pool.wait_ge(pg_mm, g * 6 + 3 * j + 3)
                    split_piece(g * 2 + 82 + j, g + 42, j, wha[:, j], wla[:, j])
                    pool.wait_ge(pj_ld[j], g * 16 + 16)
                    pool.sem_inc(spare, 1)
                    nc.gpsimd.tensor_copy(pjh[:, j], pjr[:, j]).then_inc(pool_own2, 1)
                    pool.wait_ge(pool_own2, g * 2 + j + 1)
                    nc.gpsimd.tensor_tensor(pjl[:, j], pjr[:, j], pjh[:, j].bitcast(F32), ALU.subtract).then_inc(pj_split, 1)
            end_phase(pool)

        @block.scalar
        def _(act):
            act.wait_ge(consts, 1)
            act.sem_inc(xn_done, 2)
            act.sem_inc(xt_done, 2)
            act.sem_inc(xlo_done, 2)
            act.sem_inc(w_lo1, PIECES)
            act.sem_inc(unit_out, 3)
            for i in range(3):
                act.sem_inc(unit_st[i], 16)

            def squares(s, rows, n, k):
                act.wait_ge(x_in[s], 16 * k)
                act.wait_ge(xt_done, n + 1)
                nc.scalar.activation(xn[0:rows, s], xt[0:rows, s], ACT.Square,
                                     accum_out=ssq[0:rows, s:s + 1]).then_inc(ssum_done, 1)
                act.wait_ge(ssum_done, n + 1)
                nc.scalar.activation(ssq[0:rows, s:s + 1], ssq[0:rows, s:s + 1], ACT.Sqrt, scale=1.0 / D,
                                     bias=epsc[0:rows, 0:1]).then_inc(sq_done, 1)

            def high_parts(s, rows, n, c0):
                act.wait_ge(xt_done, n + 3)
                for b in range(2):
                    nc.scalar.copy(acth[:, 4 * b:4 * b + 4, bass.ds(c0, rows)],
                                   BANK[2 * s + b][:, :].rearrange("p (k t) -> p k t", k=4)[:, :, 0:rows]).then_inc(xhi_done, 1)

            with act.Fori(0, NCH // 2) as g:
                for s in range(2):
                    squares(s, P, 2 * g + s, g + 1)
                for s in range(2):
                    high_parts(s, P, 2 * g + s, act.snap(g * 256 + s * P))
            squares(0, NS, NCH, NCH // 2 + 1)
            high_parts(0, NS, NCH, SEQ)
            act.wait_ge(wg_in, 48)
            nc.scalar.copy(wgh[:], wg[:]).then_inc(wg_hi, 1)

            def split_group(g, half):
                for j in range(PIECES):
                    act.wait_ge(w_in1[j], 32 * g + 16 * half + 16)
                    nc.scalar.copy(wh1[:, half, 2 * j:2 * j + 2, :], wraw[:, j]).then_inc(w_hi1, 1)

            def unit_evac(g, u, rows):
                act.wait_ge(unit_mm, g * 18 + u + 1)
                act.wait_ge(unit_st[u % 3], g * 96 + 16 * (u // 3) + 16)
                nc.scalar.copy(stage[0:rows, u % 3], BANK[u % 3][0:rows, :]).then_inc(unit_out, 1)

            split_group(0, 0)
            act.wait_ge(gate_x, 1)
            nc.scalar.activation(gt[:], gx[:], ACT.Abs).then_inc(act_own, 1)
            act.wait_ge(act_own, 1)
            nc.scalar.activation(gt[:], gt[:], ACT.Exp, scale=-1.0).then_inc(act_own, 1)
            act.wait_ge(act_own, 2)
            nc.scalar.activation(gt[:], gt[:], ACT.Ln, bias=1.0).then_inc(gate_l, 1)
            split_group(0, 1)
            with act.Fori(0, GROUPS // 2 - 1) as g:
                for u in range(18):
                    unit_evac(g, u, trows(u % XTILES))
                    if u == 8:
                        split_group(g + 1, 0)
                    if u == 17:
                        split_group(g + 1, 1)
            for u in range(18):
                unit_evac(GROUPS // 2 - 1, u, trows(u % XTILES))
            end_phase(act)

            act.sem_inc(f_lo, 3)
            act.sem_inc(f_mm, 9)
            act.sem_inc(f_out, 1)
            for j in range(3):
                act.sem_inc(f_st[j], 16)
            act.sem_inc(us_mm, 1)
            act.sem_inc(head_done, 1)
            act.sem_inc(h_st, 48)
            act.sem_inc(v_lo, 1)
            act.sem_inc(tqk_mm, 1)
            act.sem_inc(nb_done, 8)
            act.sem_inc(tp_mm, 8)
            act.sem_inc(pv_mm, 4)
            act.sem_inc(y_done, 2)
            act.sem_inc(y_st, 16)
            act.sem_inc(k_st, 16)
            begin_phase(act, 2)

            def gate_high(g, j, per, past=0):
                act.wait_ge(fw_in[j], 16 * (g + past) + 16)
                act.wait_ge(f_mm, 3 * per * g + 9 * past + (3 * j + 3 if per == 3 else 9))
                nc.scalar.copy(fwh[:, j], fraw[:, j]).then_inc(f_hi, 1)

            def gate_out(g, f, per, past=0):
                act.wait_ge(f_mm, 3 * per * g + 9 * past + f + 1 + 9)
                if f % 3 == 0:
                    act.wait_ge(f_st[f // 3], 16 * (g + past) + 16)
                nc.scalar.copy(fout[:, f // 3, f % 3 * TW:(f % 3 + 1) * TW], BANK[f % 2][:, 0:TW]).then_inc(f_out, 1)

            def gate_store(g, f, per, row, past=0):
                row = act.snap(row)
                act.wait_ge(f_out, 3 * per * g + 9 * past + f + 2)
                act.dma_start(o["zT"][bass.ds(row, P), :], fout[:, f // 3, :]).then_inc(f_st[f // 3], 16)

            def act_mlstm(g, last):
                act.wait_ge(rows_in, 48 * g + 48)
                nc.scalar.activation(aB[:], aB[:], ACT.Exp)
                nc.scalar.activation(nmB[:], nmB[:], ACT.Exp).then_inc(wint_done, 1)
                act.wait_ge(tq_mm, g + 1)
                nc.scalar.copy(qT[:, 0:SEQ], pA[:])
                nc.scalar.copy(qT[:, SEQ:], pS[:, 0:NS])
                nc.scalar.mul(kT[:, SEQ:], pS[:, NS:2 * NS], DM ** -0.5)
                nc.scalar.mul(kT[:, 0:SEQ], pB[:], DM ** -0.5).then_inc(qkt_done, 1)
                act.wait_ge(rm_done, g + 1)
                nc.scalar.activation(rB[:, 0:SEQ], rB[:, 0:SEQ], ACT.Exp)
                nc.scalar.activation(rB[0:NS, SEQ:], rB[0:NS, SEQ:], ACT.Exp, bias=gcur[0:NS, NCH:NCH + 1]).then_inc(e_done, 1)
                gate_high(g, 1, 3)
                gate_out(g, 0, 3)
                gate_out(g, 1, 3)
                gate_high(g, 2, 3)
                for f in range(2, 9):
                    gate_out(g, f, 3)
                    if f % 3 == 2:
                        gate_store(g, f, 3, g * P if f == 2 else (HM + g * 2 + f // 3 - 1) * P)
                    if f == 3:
                        act.wait_ge(den_mm, g + 1)
                        nc.scalar.activation(dd[:, SEQ:], pS[:, NS:2 * NS], ACT.Abs)
                        nc.scalar.activation(dd[:, 0:SEQ], pB[:], ACT.Abs).then_inc(abs_done, 1)
                    if f == 4:
                        row = act.snap(g * P)
                        act.wait_ge(h_done, g + 1)
                        act.dma_start(o["hT"][bass.ds(row, P), :], hb[:]).then_inc(h_st, 16)
                        h = act.snap(g + 0)
                        act.dma_start(o["C_prompt"][0, 0][bass.ds(h, 1)].rearrange("a d e -> (a d) e"), states[:, NCH - 1, :]).then_inc(h_st, 16)
                    if f == 5 and not last:
                        gate_high(g + 1, 0, 3)
                h = act.snap(g + 0)
                act.wait_ge(head_done, g + 2)
                act.dma_start(o["C_sample"][0][:, bass.ds(h, 1)].rearrange("b a d e -> d (b a) e"), cnew[:]).then_inc(h_st, 16)

            gate_high(0, 0, 3)
            with act.Fori(0, HM - 1) as g:
                act_mlstm(g, False)
            act_mlstm(HM - 1, True)
            act.wait_ge(h_st, 48 * (HM + 1))
            for j in range(3):
                act.wait_ge(f_st[j], 16 * (HM + 1))
            end_phase(act)

            begin_phase(act, 3)

            def squares3(g):
                act.wait_ge(qkv3_in, 48 * g + 48)
                act.wait_ge(tqk_mm, g + 1)
                act.wait_ge(k_st, 16 * g + 16)
                nc.scalar.activation(qn[:, :, 0, :], q3[:], ACT.Square)
                nc.scalar.activation(kn[:, :, 0, :], k3[:], ACT.Square).then_inc(sq3, 1)

            def rsqrt3(g):
                act.wait_ge(ms3, g + 1)
                nc.scalar.activation(ss[:, 1, :], ss[:, 0, :], ACT.Ln).then_inc(act_own, 1)
                act.wait_ge(act_own, g + 1 + 2)
                nc.scalar.activation(ss[:, 1, :], ss[:, 1, :], ACT.Exp, scale=-0.5).then_inc(rs3, 1)

            def exp3(g, i):
                act.wait_ge(nb_done, 8 * g + i + 1 + 8)
                l = lg[:, i % 2, 0:(i + 1) * P]
                nc.scalar.activation(l, l, ACT.Exp, bias=nb[:, i:i + 1]).then_inc(p_done, 1)

            def high3(g, i):
                act.wait_ge(tp_mm, 8 * g + i + 1 + 8)
                nc.scalar.copy(pt_view(pth, i), tp_bank(i)).then_inc(pt_hi, 1)

            def load_next(g):
                c = act.snap(g * DH)
                act.wait_ge(v_lo, g + 1)
                for q, buf in ((3, q3), (4, k3), (5, v3)):
                    act.dma_start(buf[:], zA_v[q][0:SEQ, bass.ds(c, DH)].rearrange("(i p) d -> p i d", p=P)).then_inc(qkv3_in, 16)

            def act_head(g, last):
                c = act.snap(g * DH)
                act.wait_ge(norm3, g + 1)
                act.dma_start(o["k_prompt"][0, 0].rearrange("(i p) h d -> p i (h d)", p=P)[:, :, bass.ds(c, DH)], kn[:, :, 0, :]).then_inc(k_st, 16)
                act.wait_ge(tqk_mm, g + 2)
                nc.scalar.copy(qst[:], pA[:]).then_inc(qk_hi, 1)
                nc.scalar.copy(khh[:], pB[:]).then_inc(qk_hi, 1)
                act.wait_ge(pv_mm, 4 * g + 4)
                nc.scalar.copy(vh[:, :, 0:DH], v3[:]).then_inc(v_hi, 1)
                exp3(g, 0)
                exp3(g, 1)
                gate_out(g, 0, 1, HM)
                if not last:
                    load_next(g + 1)
                high3(g, 0)
                exp3(g, 2)
                high3(g, 1)
                exp3(g, 3)
                high3(g, 2)
                high3(g, 3)
                exp3(g, 4)
                high3(g, 4)
                exp3(g, 5)
                high3(g, 5)
                if not last:
                    squares3(g + 1)
                exp3(g, 6)
                if not last:
                    rsqrt3(g + 1)
                gate_out(g, 1, 1, HM)
                high3(g, 6)
                exp3(g, 7)
                high3(g, 7)
                gate_out(g, 2, 1, HM)
                if not last:
                    gate_high(g + 1, 0, 1, HM)
                gate_store(g, 2, 1, (HM + 8 + g) * P, HM)

            squares3(0)
            rsqrt3(0)
            gate_high(0, 0, 1, HM)
            with act.Fori(0, HF - 1) as g:
                act_head(g, False)
            act_head(HF - 1, True)
            act.wait_ge(y_st, 16 * (HF + 1))
            act.wait_ge(k_st, 16 * (HF + 1))
            act.wait_ge(f_st[0], 16 * (HM + HF + 1))
            end_phase(act)

            act.sem_inc(grp_done, 1)
            act.sem_inc(kt_mm, 16)
            act.sem_inc(kt_a, 2)
            act.sem_inc(kt_d, 2)
            act.sem_inc(l4_mm, 4)
            act.sem_inc(o4_mm, 1)
            act.sem_inc(p4_done, 1)
            act.sem_inc(y4_st, 16)
            begin_phase(act, 4)
            def residual_tile(i):
                act.wait_ge(x4_mm, i + 1)
                nc.scalar.copy(XR[:, :, i * P:i * P + trows(i)],
                               pA[:].rearrange("p (k t) -> p k t", t=P)[:, :, 0:trows(i)]).then_inc(x4_a, 1)

            act.wait_ge(s4_in, 48)
            nc.scalar.activation(sq4b[:], qk4[:], ACT.Square).then_inc(sq4, 1)
            act.wait_ge(ms4, 1)
            nc.scalar.activation(ss4[:, 1, :], ss4[:, 0, :], ACT.Ln).then_inc(act_own, 1)
            act.wait_ge(act_own, 1 + 2 + HF)
            nc.scalar.activation(ss4[:, 1, :], ss4[:, 1, :], ACT.Exp, scale=-0.5).then_inc(rs4, 1)
            act.wait_ge(qk4_done, 1)
            act.dma_start(o["k_sample"][0].rearrange("b s h d -> (b s) (h d)"), qk4[:, 1].rearrange("t h d -> t (h d)")).then_inc(k4_st, 16)
            for i in range(0, XTILES, 2):
                residual_tile(i)
            for s in reused:
                act.sem_clear(s)
            for s, n in ((w_split, 2), (b_done, 6), (a_mm, 12), (t_done, 6), (o_mm, 6), (x5_done, 3), (ss5_mm, 3), (gu_mm, 6), (un_done, 2),
                         (dn_mm, 24), (x6_done, 4), (pj_split, 2), (ss7_mm, 3), (pg_mm, 6), (y7_done, 2), (yt_mm, 2), (yt_out, 1),
                         (y7_st[0], 32), (y7_st[1], 32)):
                act.sem_inc(s, n)
            act.sem_inc(cleared, 1)
            with act.Fori(0, DB // GB) as g:
                for s in range(0, 16, 2):
                    act.wait_ge(l4_mm, 16 * g + s + 1)
                    act.wait_ge(kt_mm, 16 * g + s + 1 + 16)
                    nc.scalar.copy(ktp[:, s % 4, :], kt_bank(s)).then_inc(kt_a, 1)
                act.wait_ge(nb4, g + 1)
                nc.scalar.activation(px[:], pC[:, 0:PAGES * PAGE + NS], ACT.Exp, bias=mx4[:, 2:3]).then_inc(e4_done, 1)
                act.wait_ge(o4_mm, g + 2)
                nc.scalar.copy(px[:, 0:W], BANK[0][:]).then_inc(o4_out, 1)
                c = act.snap(g * (GB * DS) + SEQ)
                act.wait_ge(y4_done, g + 1)
                act.dma_start(o["yT"].rearrange("(c p) t -> p c t", p=P)[:, :, bass.ds(c, GB * DS)],
                              ysg[:].rearrange("p c b t -> p c (b t)")).then_inc(y4_st, 16)
            act.wait_ge(y4_st, 16 * (DB // GB + 1))
            act.wait_ge(k4_st, 16)
            end_phase(act)

            begin_phase(act, 5)
            for c in range(4):
                if c % 2 == 0:
                    act.wait_ge(y5_in[c // 2], 16)
                nc.scalar.copy(acth[:, 4 + c, :], yst5[:, c, :]).then_inc(y5_hi, 1)
            def sigmoid5(c):
                act.wait_ge(g5_in[c % 2], 16 * (c // 2) + 16)
                nc.scalar.activation(gs[:, c % 2, :], gs[:, c % 2, :], ACT.Sigmoid).then_inc(g5_sig, 1)

            sigmoid5(0)
            sigmoid5(1)
            act.wait_ge(mo5_in, 16)
            for h in range(HM):
                nc.scalar.activation(mo5[:, h, :], mo5[:, h, :], ACT.Sigmoid).then_inc(mo_sig, 1)
            act.wait_ge(h5_in, 16)
            for h in range(HM):
                nc.scalar.activation(rvm[:, h, :], hst5[:, h, :], ACT.Square).then_inc(hsq, 1)
            sigmoid5(2)
            sigmoid5(3)
            for n in range(HM * NT):
                h, t = n // NT, n % NT
                act.wait_ge(hss_mm, n + 1)
                nc.scalar.activation(rvm[:, h, t * TW:(t + 1) * TW], BANK[4 + n % 4][:, 0:TW], ACT.Ln, scale=1.0 / DM, bias=epsc[:]).then_inc(hln, 1)
            for h in range(HM):
                act.wait_ge(hln, NT * h + NT)
                nc.scalar.activation(rvm[:, h, :], rvm[:, h, :], ACT.Exp, scale=-0.5).then_inc(hrv, 1)
            sigmoid5(4)
            for h in range(HM):
                act.wait_ge(hm_done, h + 1)
                nc.scalar.copy(acth[:, h, :], rvm[:, h, :]).then_inc(hm_hi, 1)
                if h < 3:
                    sigmoid5(5 + h)
            with act.Fori(0, 2) as g:
                for c in range(4):
                    act.wait_ge(g5_in[c % 2], g * 32 + 16 * (c // 2) + 80)
                    nc.scalar.activation(gs[:, c % 2, :], gs[:, c % 2, :], ACT.Sigmoid).then_inc(g5_sig, 1)
                    for t in range(NT):
                        act.wait_ge(t_done, g * 12 + 3 * c + t + 1 + 6)
                        act.sem_inc(spare, 1)
                        nc.scalar.copy(th[:, bass.ds(g * 4 + c, 1), t * TW:(t + 1) * TW].rearrange("p a t -> p (a t)"), tmp[:, t, :]).then_inc(t_hi, 1)
            act.wait_ge(gv_in, 48)
            with act.Fori(0, KC // 2) as g:
                for j in range(2):
                    for t in range(NT):
                        u = 3 * j + t
                        cols = slice(t * TW, (t + 1) * TW)
                        act.wait_ge(x5_done, g * 6 + u + 1 + 3)
                        act.sem_inc(spare, 1)
                        act.wait_ge(ss5_mm, g * 6 + u + 1)
                        act.sem_inc(spare, 1)
                        x = XR[:, bass.ds(g * 2 + j, 1), cols].rearrange("p a t -> p (a t)")
                        nc.scalar.activation(sqt[:, t, :], x, ACT.Square).then_inc(sq5, 1)
                        nc.scalar.activation(acth[:, bass.ds(g * 2 + j, 1), cols].rearrange("p a t -> p (a t)"), x, ACT.Identity,
                                             scale=gc[:, j:j + 1]).then_inc(xg_hi, 1)
            for t in range(NT):
                act.wait_ge(ss5_mm, 3 + 3 * KC + NT)
                nc.scalar.activation(rv[:, t, :], BANK[4 + t][:, 0:TW], ACT.Ln, scale=1.0 / D, bias=epsc[:]).then_inc(act_own, 1)
            for t in range(NT):
                act.wait_ge(act_own, 3 + HF + t + 1)
                nc.scalar.activation(rv[:, t, :], rv[:, t, :], ACT.Exp, scale=-0.5).then_inc(rv_done, 1)

            with act.Fori(0, NFF // 2) as g:
                for v in range(6):
                    j, t = v // 3, v % 3
                    act.wait_ge(gn_done, g * 6 + v + 1)
                    nc.scalar.activation(gn[:, v % 2, :], gn[:, v % 2, :], ACT.Silu).then_inc(sl_done, 1)
                    act.wait_ge(dn_mm, g * 24 + 8 * t + 8)
                    act.wait_ge(hd_done, g * 6 + v + 1)
                    nc.scalar.copy(hh[:, j, t * TW:(t + 1) * TW], un[:, v % 2, :]).then_inc(h_hi, 1)

            act.wait_ge(x6_done, 4 + 12 * NFF)
            for n in range(NT * KC):
                t, c = n // KC, n % KC
                cols = slice(t * TW, (t + 1) * TW)
                if n == KC:
                    for k in range(2):
                        act.wait_ge(pt7_mm, k + 1)
                        nc.scalar.copy(pTh[:, k, SEQ:], BANK[k][:, 0:NS])
                        nc.scalar.copy(pTh[:, k, 0:SEQ], PAIR[2 * k][:]).then_inc(pt7_hi, 1)
                nc.scalar.activation(acth[:, c, cols], XR[:, c, cols], ACT.Identity, scale=gv[:, HM + KC + c:HM + KC + c + 1]).then_inc(xp_hi, 1)
            for t in range(NT):
                act.wait_ge(ss7_mm, 3 + KC * t + KC)
                nc.scalar.activation(rv[:, t, :], BANK[4 + t][:, 0:TW], ACT.Ln, scale=1.0 / D, bias=epsc[:]).then_inc(act_own, 1)
            for t in range(NT):
                act.wait_ge(act_own, 6 + HF + t + 1)
                nc.scalar.activation(rv[:, t, :], rv[:, t, :], ACT.Exp, scale=-0.5).then_inc(rv7_done, 1)
            with act.Fori(0, KC // 2) as g:
                for v in range(6):
                    act.wait_ge(pgn, g * 6 + v + 1)
                    nc.scalar.activation(gn[:, v % 2, :], gn[:, v % 2, :], ACT.Sigmoid).then_inc(sg7, 1)
                for j in range(2):
                    c = act.snap(g * 256 + j * P)
                    act.wait_ge(y7_st[j], g * 32 + 32)
                    act.wait_ge(yt_mm, g * 2 + j + 1 + 2)
                    nc.scalar.copy(yst7[0:NS, j, NCH, :], BANK[6][0:NS, 0:P])
                    nc.scalar.copy(yst7[:, j, 0:NCH, :].rearrange("p i n -> p (i n)"), PAIR[1][:]).then_inc(yt_out, 1)
                    act.wait_ge(yt_out, g * 2 + j + 2)
                    act.dma_start(o["y_prompt"][0].rearrange("(i p) n -> p i n", p=P)[:, :, bass.ds(c, P)], yst7[:, j, 0:NCH, :]).then_inc(y7_st[j], 16)
                    act.dma_start(o["y_sample"].rearrange("b s n -> (b s) n")[:, bass.ds(c, P)], yst7[0:NS, j, NCH, :]).then_inc(y7_st[j], 16)
            for j in range(2):
                act.wait_ge(y7_st[j], 32 * (KC // 2) + 32)
            end_phase(act)

        @block.vector
        def _(dve):
            own = Chain(dve, dve_own)

            def norm(s, rows, n):
                dve.wait_ge(sq_done, n + 1)
                own.step(nc.vector.reciprocal(ssq[0:rows, 2 + s:3 + s], ssq[0:rows, s:s + 1]))
                nc.vector.scalar_tensor_tensor(out=xn[0:rows, s], in0=xt[0:rows, s], scalar=ssq[0:rows, 2 + s:3 + s],
                                               in1=gmix[0:rows, :], op0=ALU.mult, op1=ALU.mult).then_inc(xn_done, 1)

            def low_parts(s, rows, n, c0):
                for b in range(2):
                    dve.wait_ge(xhi_done, 2 * n + b + 1)
                    ins = nc.vector.tensor_tensor(actl[:, 4 * b:4 * b + 4, bass.ds(c0, rows)],
                                                  BANK[2 * s + b][:, :].rearrange("p (k t) -> p k t", k=4)[:, :, 0:rows],
                                                  acth[:, 4 * b:4 * b + 4, bass.ds(c0, rows)].bitcast(F32), ALU.subtract)
                ins.then_inc(xlo_done, 1)

            dve.wait_ge(small_in, 80)
            with dve.Fori(0, NCH // 2) as g:
                own.enter(g, 2)
                for s in range(2):
                    norm(s, P, 2 * g + s)
                for s in range(2):
                    low_parts(s, P, 2 * g + s, dve.snap(g * 256 + s * P))
                own.leave(NCH // 2)
            norm(0, NS, NCH)
            low_parts(0, NS, NCH, SEQ)

            dve.wait_ge(gate_mm, 1)
            nc.vector.memset(keep[:], 1.0)
            own.step(nc.vector.memset(rr[:], 0.0))
            nc.vector.memset(keep[:, 0:SEQ:P], 0.0)
            own.step(nc.vector.memset(keep[:, SEQ::DS], 0.0))
            for t in range(NT):
                ins = nc.vector.tensor_scalar(gx[:, t * TW:(t + 1) * TW], BANK[5 + t][0:GW, 0:TW], gbias[:, 0:1], None, ALU.add)
            ins.then_inc(gate_x, 1)
            dve.wait_ge(gate_l, 1)
            own.step(nc.vector.scalar_tensor_tensor(out=glf[:], in0=gx[:], scalar=0.0, in1=gt[:], op0=ALU.min, op1=ALU.subtract))
            own.step(nc.vector.tensor_copy(mlf[:], glf[32:32 + HM, :]))
            own.step(nc.vector.tensor_tensor_scan(b_row, keep[:], mlf[:], 0.0, ALU.mult, ALU.add))
            own.step(nc.vector.tensor_tensor(rr[0:HM, :], gx[0:HM, :], b_row, ALU.subtract))
            own.step(nc.vector.tensor_copy(lfm[:], mlf[:]))
            own.step(nc.vector.tensor_copy(igm[:], gx[0:HM, :]))
            own.step(nc.vector.tensor_tensor(smt[:], mlf[:, SEQ::DS], sm[:], ALU.add))
            own.step(nc.vector.tensor_tensor(igm[:, SEQ::DS], smt[:], gx[0:HM, SEQ::DS], ALU.max))
            own.step(nc.vector.memset(lfm[:, SEQ::DS], NEG))
            own.step(nc.vector.tensor_tensor_scan(m_row[:], lfm[:], igm[:], 0.0, ALU.add, ALU.max))
            own.step(nc.vector.memset(ms_row[:, 0:P], 0.0))
            own.step(nc.vector.tensor_copy(ms_row[:, P:SEQ].rearrange("h (c t) -> h c t", t=P),
                                           m_row[:, P - 1:SEQ - 1:P].unsqueeze(2).to_broadcast([HM, NCH - 1, P])))
            own.step(nc.vector.tensor_copy(ms_row[:, SEQ:].rearrange("h (b t) -> h b t", t=DS),
                                           sm[:].unsqueeze(2).to_broadcast([HM, DB, DS])))
            own.step(nc.vector.tensor_tensor(lfm[:], b_row, m_row[:], ALU.subtract))
            own.step(nc.vector.tensor_tensor(igm[:], lfm[:], ms_row[:], ALU.add))
            own.step(nc.vector.tensor_scalar(mlf[:], m_row[:], -1.0, None, ALU.mult))
            own.step(nc.vector.tensor_copy(rr[64:64 + HF, :], glf[64:64 + HF, :]))
            own.step(nc.vector.tensor_tensor_scan(gx[64:64 + HF, 0:SEQ], ones[64:64 + HF, 0:1].to_broadcast([HF, SEQ]),
                                                  glf[64:64 + HF, 0:SEQ], 0.0, ALU.mult, ALU.add))
            own.step(nc.vector.memset(gx[64:64 + HF, SEQ:], 0.0))
            own.step(nc.vector.tensor_scalar(gt[64:64 + HF, :], gx[64:64 + HF, :], -1.0, None, ALU.mult))
            nc.vector.tensor_copy(rr[32:32 + HF, :], gx[64:64 + HF, :]).then_inc(rows_done, 1)
            dve.wait_ge(col_mm, 1)
            nc.vector.tensor_copy(col[:, 0:5, :], BANK[3][:, 0:5 * GW].rearrange("p (c n) -> p c n", c=5))
            nc.vector.tensor_copy(col[:, 5:8, :], BANK[4][:, 0:3 * GW].rearrange("p (c n) -> p c n", c=3))
            nc.vector.tensor_copy(col[0:NS, 8, :], BANK[4][0:NS, 3 * GW:4 * GW]).then_inc(col_done, 1)
            end_phase(dve)

            begin_phase(dve, 2)
            dve.wait_ge(nst_t, 1)
            own.step(nc.vector.tensor_copy(nst[:], pN[:, 0:DB * HM]))
            with dve.Fori(0, HM) as g:
                own.enter(g, 13)
                nst_v = nst[:].rearrange("p (b h) -> p b h", h=HM)
                dve.wait_ge(head_done, g + 1)
                own.step(nc.vector.tensor_scalar(ncur[:].unsqueeze(2), nst_v[:, :, bass.ds(g, 1)], 1.0, None, ALU.mult))
                nc.vector.tensor_scalar(gcur[0:NS, NCH:], col[0:NS, NCH, bass.ds(g, 1)], 1.0, None, ALU.mult)
                nc.vector.tensor_scalar(gcur[:, 0:NCH].unsqueeze(2), col[:, 0:NCH, bass.ds(g, 1)], 1.0, None, ALU.mult).then_inc(gcur_done, 1)
                dve.wait_ge(qkt_done, g + 1)
                nc.vector.tensor_tensor(qs[:], qT[:], aB[:], ALU.mult).then_inc(qs_done, 1)
                dve.wait_ge(e_done, g + 1)
                dve.wait_ge(qkv_in, 96 * g + 96)
                nc.vector.scalar_tensor_tensor(out=kws[:], in0=k_in[0:NS, NCH:NCH + 1, :].to_broadcast([NS, DB, DM]), scalar=DM ** -0.5,
                                               in1=rB[0:NS, SEQ + DS - 1::DS].unsqueeze(2).to_broadcast([NS, DB, DM]),
                                               op0=ALU.mult, op1=ALU.mult)
                nc.vector.scalar_tensor_tensor(out=kw[:], in0=k_in[:, 0:NCH, :], scalar=DM ** -0.5,
                                               in1=rB[:, P - 1:SEQ:P].unsqueeze(2).to_broadcast([P, NCH, DM]),
                                               op0=ALU.mult, op1=ALU.mult).then_inc(kw_done, 1)
                dve.wait_ge(s_mm, g + 1)
                nc.vector.tensor_tensor(sw[0:NS, SEQ:], pS[0:NS, 0:NS], rB[0:NS, SEQ:], ALU.mult)
                nc.vector.tensor_tensor(sw[:, 0:SEQ], pA[:], rB[:, 0:SEQ], ALU.mult).then_inc(sw_done, 1)
                dve.wait_ge(h_st, 48 * g + 48)
                dve.wait_ge(u_mm, g + 1)
                own.step(nc.vector.tensor_tensor_scan(nstates[:], aB[:, P - 1:SEQ:P], pN[:, 0:NCH], 0.0, ALU.mult, ALU.add))
                own.step(nc.vector.tensor_copy(states[:, 0, :], pB[:, 0:DM]))
                for c in range(1, NCH):
                    ins = nc.vector.scalar_tensor_tensor(out=states[:, c, :], in0=states[:, c - 1, :], scalar=aB[:, c * P + P - 1:c * P + P],
                                                         in1=pB[:, c * DM:(c + 1) * DM], op0=ALU.mult, op1=ALU.add)
                    if c < NCH - 1:
                        own.step(ins)
                ins.then_inc(c_done, 1)
                dve.wait_ge(cs_in, 16 * g + 16)
                decay = aB[:, SEQ + DS - 1::DS]
                nc.vector.tensor_tensor(cnew[:], cst[:], decay.unsqueeze(2).to_broadcast([P, DB, DM]), ALU.mult)
                nc.vector.tensor_tensor(nnew[:], ncur[:], decay, ALU.mult)
                dve.wait_ge(abs_done, g + 1)
                own.step(nc.vector.tensor_tensor(dd[:], dd[:], nmB[:], ALU.max))
                own.step(nc.vector.reciprocal(dd[:], dd[:]))
                nc.vector.tensor_tensor(hb[:, SEQ:], pS[:, 0:NS], dd[:, SEQ:], ALU.mult)
                nc.vector.tensor_tensor(hb[:, 0:SEQ], pA[:], dd[:, 0:SEQ], ALU.mult).then_inc(h_done, 1)
                dve.wait_ge(us_mm, g + 2)
                nc.vector.tensor_scalar(nout[:, bass.ds(g, 1)], nstates[:, NCH - 1:NCH], 1.0, None, ALU.mult)
                own.step(nc.vector.tensor_tensor(nnew[:], nnew[:], pN[:, NCH:NCH + DB], ALU.add))
                own.step(nc.vector.tensor_scalar(nout[:, HM:].rearrange("p (b h) -> p b h", h=HM)[:, :, bass.ds(g, 1)], nnew[:].unsqueeze(2), 1.0, None, ALU.mult))
                nc.vector.tensor_tensor(cnew[:], cnew[:], pA[:].rearrange("p (b e) -> p b e", e=DM), ALU.add).then_inc(head_done, 1)
                own.leave(HM)
            dve.wait_ge(n_mm, 1)
            nc.vector.tensor_copy(nrow[:], pN[0:HM * (DB + 1), 0:P]).then_inc(n_done, 1)
            end_phase(dve)

            begin_phase(dve, 3)
            dve.wait_ge(g_in, 32)
            nc.vector.tensor_scalar(gqk[:, 0, :], gqk[:, 0, :], DH ** -0.5, None, ALU.mult).then_inc(g_done, 1)

            def mean3(g):
                dve.wait_ge(sq3, g + 1)
                nc.vector.tensor_reduce(ss[:, 0, 0:NCH], qn[:, :, 0, :], AX.X, ALU.add)
                own.step(nc.vector.tensor_reduce(ss[:, 0, NCH:], kn[:, :, 0, :], AX.X, ALU.add))
                nc.vector.tensor_scalar(ss[:, 0, :], ss[:, 0, :], 1.0 / DH, EPS, ALU.mult, ALU.add).then_inc(ms3, 1)

            def refine3(g):
                dve.wait_ge(rs3, g + 1)
                x, y, t = ss[:, 0, :], ss[:, 1, :], ss[:, 2, :]
                own.step(nc.vector.tensor_tensor(t, y, y, ALU.mult))
                own.step(nc.vector.tensor_tensor(t, t, x, ALU.mult))
                own.step(nc.vector.tensor_scalar(t, t, -0.5, 1.5, ALU.mult, ALU.add))
                nc.vector.tensor_tensor(y, y, t, ALU.mult).then_inc(ri3, 1)

            def bias3(g, i):
                dve.wait_ge(lg_mm, 8 * g + i + 1)
                dve.wait_ge(tp_mm, 8 * g + i + 7)
                nc.vector.memset(waits[:], 0.0)
                own.step(nc.vector.tensor_tensor_reduce(out=lg[:, i % 2, 0:(i + 1) * P], in0=lg_bank(i), in1=nF[:, 0:(i + 1) * P],
                                               scale=1.0, scalar=-3.0e38, op0=ALU.add, op1=ALU.max,
                                               accum_out=mx[:, i:i + 1]))
                f = colF(i)
                nc.vector.scalar_tensor_tensor(out=nb[:, i:i + 1], in0=mx[:, i:i + 1], scalar=f, in1=f,
                                               op0=ALU.add, op1=ALU.subtract, reverse1=True).then_inc(nb_done, 1)

            def low3(g, i):
                dve.wait_ge(pt_hi, 8 * g + i + 1)
                nc.vector.tensor_tensor(pt_view(ptl, i), tp_bank(i), pt_view(pth, i).bitcast(F32), ALU.subtract).then_inc(pt_lo, 1)

            def out3(g, m):
                b = m // 2
                dve.wait_ge(pv_mm, 4 * g + 2 * b + 2 + 4)
                if m == 0:
                    dve.wait_ge(y_st, 16 * g + 16)
                y = yb[:, m * 256:(m + 1) * 256]
                own.step(nc.vector.reciprocal(y, pC[DH:, m * 256:(m + 1) * 256]))
                ins = nc.vector.tensor_tensor(y, pC[0:DH, m * 256:(m + 1) * 256], y, ALU.mult)
                if m % 2:
                    ins.then_inc(y_done, 1)

            def dve_head(g, first, last):
                dve.wait_ge(qk_hi, 2 * g + 1)
                nc.vector.tensor_scalar(fcol[:].unsqueeze(2), col[:, 0:NCH, bass.ds(32 + g, 1)], 1.0, None, ALU.mult)
                own.step(nc.vector.tensor_tensor(qst[DH:, :], pA[DH:, :], qst[DH:, :].bitcast(F32), ALU.subtract))
                dve.wait_ge(qk_hi, 2 * g + 2)
                nc.vector.tensor_tensor(klo[:], pB[0:DH, :], khh[0:DH, :].bitcast(F32), ALU.subtract).then_inc(qk_lo, 1)
                dve.wait_ge(nF_in, 16 * g + 16)
                bias3(g, 0)
                bias3(g, 1)
                if not first:
                    out3(g - 1, 2)
                bias3(g, 2)
                low3(g, 0)
                bias3(g, 3)
                low3(g, 1)
                low3(g, 2)
                bias3(g, 4)
                low3(g, 3)
                if not first:
                    out3(g - 1, 3)
                bias3(g, 5)
                low3(g, 4)
                out3(g, 0)
                bias3(g, 6)
                low3(g, 5)
                if not last:
                    mean3(g + 1)
                bias3(g, 7)
                if not last:
                    refine3(g + 1)
                low3(g, 6)
                out3(g, 1)
                low3(g, 7)

            mean3(0)
            refine3(0)
            dve_head(0, True, False)
            with dve.Fori(0, HF - 2) as g:
                own.enter(g, 1 + 8 + 4 + 4)
                dve_head(g + 1, False, False)
                own.leave(HF - 2)
            dve_head(HF - 1, False, True)
            out3(HF - 1, 2)
            out3(HF - 1, 3)
            end_phase(dve)

            begin_phase(dve, 4)
            dve.wait_ge(sq4, 1)
            own.step(nc.vector.tensor_reduce(ss4[:, 0, :], sq4b[:].rearrange("t j h d -> t (j h) d"), AX.X, ALU.add))
            nc.vector.tensor_scalar(ss4[:, 0, :], ss4[:, 0, :], 1.0 / DH, EPS, ALU.mult, ALU.add).then_inc(ms4, 1)
            own.step(nc.vector.tensor_scalar(mc01[:], maskS[:], 1.0, 0.0, ALU.add, ALU.max))
            nc.vector.tensor_scalar(nmc[:], mc01[:], -1.0, None, ALU.mult)
            nc.vector.tensor_copy(lf4[:], col[0:NS, NCH, 64:64 + HF].unsqueeze(2).to_broadcast([NS, HF, DS]))
            nc.vector.memset(qz[:], 0.0)
            dve.wait_ge(rs4, 1)
            x, y, t = ss4[:, 0, :], ss4[:, 1, :], ss4[:, 2, :]
            own.step(nc.vector.tensor_tensor(t, y, y, ALU.mult))
            own.step(nc.vector.tensor_tensor(t, t, x, ALU.mult))
            own.step(nc.vector.tensor_scalar(t, t, -0.5, 1.5, ALU.mult, ALU.add))
            own.step(nc.vector.tensor_tensor(y, y, t, ALU.mult))
            qk_v = qk4[:].rearrange("t j h d -> t (j h) d")
            own.step(nc.vector.tensor_tensor(qk_v, qk_v, y.unsqueeze(2).to_broadcast([NS, 2 * HF, DH]), ALU.mult))
            nc.vector.tensor_tensor(qk4[:], qk4[:], gqk[0:NS].unsqueeze(2).to_broadcast([NS, 2, HF, DH]), ALU.mult).then_inc(qk4_done, 1)
            for i in range(1, XTILES, 2):
                dve.wait_ge(x4_mm, i + 1)
                nc.vector.tensor_copy(XR[:, :, i * P:(i + 1) * P], pB[:].rearrange("p (k t) -> p k t", t=P)).then_inc(x4_d, 1)
            dve.wait_ge(tq4_mm, 1)
            nc.vector.tensor_copy(qT4[:].rearrange("p c t -> p (c t)"), BANK[0][:, 0:P])
            own.step(nc.vector.tensor_copy(kT4[:].rearrange("p c t -> p (c t)"), BANK[0][:, P:2 * P]))
            with dve.Fori(0, DB // GB) as g:
                own.enter(g, 4)
                tok = bass.ds(g * (GB * DS), GB * DS)
                for c in range(4):
                    for j in range(2):
                        nc.vector.tensor_scalar(qz[j * DH:(j + 1) * DH, c, :, 2 * c + j, :],
                                                qT4[j * DH:(j + 1) * DH, c, tok].rearrange("p (b t) -> p b t", t=DS), 1.0, None, ALU.mult)
                nc.vector.tensor_scalar(sel[:], ident[0:NS, tok].rearrange("p (b t) -> p b t", t=DS).unsqueeze(2).to_broadcast([NS, GB, HF, DS]),
                                        1.0, None, ALU.mult)
                nc.vector.tensor_tensor(lfq[:], lf4[:].unsqueeze(1).to_broadcast([NS, GB, HF, DS]),
                                        mc01[:, tok].rearrange("p (b t) -> p b t", t=DS).unsqueeze(2).to_broadcast([NS, GB, HF, DS]), ALU.mult)
                dve.wait_ge(lf_ready, g + 1)
                nc.vector.tensor_scalar(lfr[:], lfp[:, bass.ds(g * (GB * PAGES), GB * PAGES), :].unsqueeze(3).to_broadcast([P, GB * PAGES, HF, DS]),
                                        1.0, None, ALU.mult).then_inc(grp_done, 1)
                for s in range(1, 16, 2):
                    dve.wait_ge(l4_mm, 16 * g + s + 1)
                    dve.wait_ge(kt_mm, 16 * g + s + 1 + 16)
                    nc.vector.tensor_copy(ktp[:, s % 4, :], kt_bank(s)).then_inc(kt_d, 1)
                dve.wait_ge(l4_mm, 16 * g + 16 + 4)
                nc.vector.tensor_reduce(mx4[:, 0:1], pC[:, 0:PAGES * PAGE + NS], AX.X, ALU.max)
                own.step(nc.vector.tensor_copy(mx4[:, 1:2], pC[:, PAGES * PAGE + NS:PAGES * PAGE + NS + 1]))
                own.step(nc.vector.tensor_tensor(mx4[:, 2:3], mx4[:, 0:1], mx4[:, 1:2], ALU.add))
                nc.vector.tensor_tensor(mx4[:, 2:3], mx4[:, 1:2], mx4[:, 2:3], ALU.subtract).then_inc(nb4, 1)
                dve.wait_ge(e4_done, g + 1)
                own.step(nc.vector.tensor_reduce(mx4[:, 3:4], px[:], AX.X, ALU.add))
                own.step(nc.vector.reciprocal(mx4[:, 3:4], mx4[:, 3:4]))
                nc.vector.tensor_scalar(px[:], px[:], mx4[:, 3:4], None, ALU.mult).then_inc(p4_done, 1)
                dve.wait_ge(tp4_mm, g + 1)
                nc.vector.tensor_copy(pT4[0:NS, PAGES, :], BANK[1][0:NS, 0:P])
                nc.vector.tensor_copy(pT4[:, 0:PAGES, :].rearrange("p a b -> p (a b)"), BANK[0][:]).then_inc(pt4_done, 1)
                dve.wait_ge(y4_st, 16 * g + 16)
                dve.wait_ge(ot4_mm, g + 1)
                out_v = BANK[1][:].rearrange("p (c b h t) -> p c b h t", c=4, b=GB, h=HF)
                for c in range(4):
                    for j in range(2):
                        ins = nc.vector.tensor_copy(ysg[j * DH:(j + 1) * DH, c], out_v[j * DH:(j + 1) * DH, c, :, 2 * c + j, :])
                ins.then_inc(y4_done, 1)
            own.leave(DB // GB)
            end_phase(dve)

            begin_phase(dve, 5)
            dve.wait_ge(cleared, 1)
            dve.sem_inc(started, 1)
            for c in range(4):
                dve.wait_ge(y5_hi, c + 1)
                nc.vector.tensor_tensor(actl[:, 4 + c, :], yst5[:, c, :], acth[:, 4 + c, :].bitcast(F32), ALU.subtract).then_inc(y5_lo, 1)

            def norm_mlstm(h):
                dve.wait_ge(hrv, h + 1)
                own.step(nc.vector.scalar_tensor_tensor(out=rvm[:, h, :], in0=hst5[:, h, :], scalar=gv[:, h:h + 1], in1=rvm[:, h, :],
                                                        op0=ALU.mult, op1=ALU.mult))
                nc.vector.tensor_tensor(rvm[:, h, :], rvm[:, h, :], mo5[:, h, :], ALU.mult).then_inc(hm_done, 1)

            def low_mlstm(h):
                dve.wait_ge(hm_hi, h + 1)
                nc.vector.tensor_tensor(actl[:, h, :], rvm[:, h, :], acth[:, h, :].bitcast(F32), ALU.subtract).then_inc(hm_lo, 1)

            dve.wait_ge(gv_in, 48)
            for c in range(KC):
                if c >= 4:
                    norm_mlstm(c - 4)
                if c >= 6:
                    low_mlstm(c - 6)
                dve.wait_ge(g5_sig, c + 1)
                for t in range(NT):
                    u = 3 * c + t
                    dve.wait_ge(b_mm, u + 1)
                    if u == 0:
                        dve.wait_ge(y5_lo, 4)
                    nc.vector.tensor_tensor(tpart[:, c, t * TW:(t + 1) * TW], BANK[u % 4][:, 0:TW], gs[:, c % 2, t * TW:(t + 1) * TW],
                                            ALU.mult).then_inc(b_done, 1)
            low_mlstm(2)
            low_mlstm(3)

            def low_t(g, u):
                c, t = u // 3, u % 3
                dve.wait_ge(t_hi, g * 12 + u + 1)
                at_c = (slice(None), bass.ds(g * 4 + c, 1), slice(t * TW, (t + 1) * TW))
                nc.vector.tensor_tensor(tl[at_c].rearrange("p a t -> p (a t)"), tmp[:, t, :],
                                        th[at_c].rearrange("p a t -> p (a t)").bitcast(F32), ALU.subtract).then_inc(t_lo, 1)

            with dve.Fori(0, 2) as g:
                own.enter(g, 12)
                for u in range(12):
                    c, t = u // 3, u % 3
                    if t == 0:
                        dve.wait_ge(g5_sig, g * 4 + c + 1 + KC)
                    dve.wait_ge(a_mm, g * 12 + u + 1 + 12)
                    own.step(nc.vector.tensor_tensor(tmp[:, t, :], BANK[u % 4][:, 0:TW], gs[:, c % 2, t * TW:(t + 1) * TW], ALU.mult))
                    nc.vector.tensor_tensor(tmp[:, t, :], tmp[:, t, :], tpart[:, bass.ds(g * 4 + c, 1), t * TW:(t + 1) * TW].rearrange("p a t -> p (a t)"),
                                            ALU.add).then_inc(t_done, 1)
                    if u > 0:
                        low_t(g, u - 1)
                low_t(g, 11)
                own.leave(2)

            nc.vector.memset(rv[:], 0.0).then_inc(rv_zero, 1)

            def low_x(g, u):
                j, t = u // 3, u % 3
                at_c = (slice(None), bass.ds(g * 2 + j, 1), slice(t * TW, (t + 1) * TW))
                dve.wait_ge(xg_hi, g * 6 + u + 1)
                nc.vector.scalar_tensor_tensor(out=actl[at_c].rearrange("p a t -> p (a t)"), in0=XR[at_c].rearrange("p a t -> p (a t)"),
                                               scalar=gc[:, j:j + 1], in1=acth[at_c].rearrange("p a t -> p (a t)").bitcast(F32),
                                               op0=ALU.mult, op1=ALU.subtract).then_inc(xg_lo, 1)

            with dve.Fori(0, KC // 2) as g:
                own.enter(g, 1)
                own.step(nc.vector.tensor_scalar(gc[:], gv[:, bass.ds(g * 2 + HM, 2)], 1.0, None, ALU.mult))
                for u in range(6):
                    j, t = u // 3, u % 3
                    dve.wait_ge(o_mm, g * 6 + u + 1 + 6)
                    x = XR[:, bass.ds(g * 2 + j, 1), t * TW:(t + 1) * TW].rearrange("p a t -> p (a t)")
                    nc.vector.tensor_tensor(x, x, BANK[u % 3][:, 0:TW], ALU.add).then_inc(x5_done, 1)
                    if u > 0:
                        low_x(g, u - 1)
                low_x(g, 5)
                dve.wait_ge(xg_lo, g * 6 + 6)
                own.leave(KC // 2)

            dve.wait_ge(rv_done, NT)
            with dve.Fori(0, NFF // 2) as g:
                def unit_hidden(v):
                    dve.wait_ge(un_done, g * 6 + v + 3)
                    dve.wait_ge(sl_done, g * 6 + v + 1)
                    nc.vector.tensor_tensor(un[:, v % 2, :], un[:, v % 2, :], gn[:, v % 2, :], ALU.mult).then_inc(hd_done, 1)

                def unit_low(v):
                    j, t = v // 3, v % 3
                    dve.wait_ge(h_hi, g * 6 + v + 1)
                    nc.vector.tensor_tensor(hl[:, j, t * TW:(t + 1) * TW], un[:, v % 2, :], hh[:, j, t * TW:(t + 1) * TW].bitcast(F32),
                                            ALU.subtract).then_inc(h_lo, 1)

                for v in range(6):
                    t = v % 3
                    dve.wait_ge(gu_mm, g * 6 + v + 1 + 6)
                    if v >= 2:
                        dve.wait_ge(h_lo, g * 6 + v - 1)
                    nc.vector.tensor_tensor(gn[:, v % 2, :], BANK[v % 2 * 2][:, 0:TW], rv[:, t, :], ALU.mult).then_inc(gn_done, 1)
                    nc.vector.tensor_tensor(un[:, v % 2, :], BANK[v % 2 * 2 + 1][:, 0:TW], rv[:, t, :], ALU.mult).then_inc(un_done, 1)
                    if v > 0:
                        unit_hidden(v - 1)
                        if v < 5:
                            unit_low(v - 1)
                unit_hidden(5)
                for u in range(24):
                    t, c = u // KC, u % KC
                    dve.wait_ge(dn_mm, g * 24 + u + 1 + 24)
                    x = XR[:, c, t * TW:(t + 1) * TW]
                    nc.vector.tensor_tensor(x, x, BANK[4 + u % 4][:, 0:TW], ALU.add).then_inc(x6_done, 1)
                    if u == 0:
                        unit_low(4)
                    if u == 1:
                        unit_low(5)
                dve.wait_ge(h_lo, g * 6 + 6)

            for n in range(NT * KC):
                t, c = n // KC, n % KC
                cols = slice(t * TW, (t + 1) * TW)
                if n == KC:
                    for k in range(2):
                        dve.wait_ge(pt7_hi, k + 1)
                        nc.vector.tensor_tensor(pTl[:, k, SEQ:], BANK[k][:, 0:NS], pTh[:, k, SEQ:].bitcast(F32), ALU.subtract)
                        nc.vector.tensor_tensor(pTl[:, k, 0:SEQ], PAIR[2 * k][:], pTh[:, k, 0:SEQ].bitcast(F32), ALU.subtract).then_inc(pt7_lo, 1)
                dve.wait_ge(xp_hi, n + 1)
                nc.vector.scalar_tensor_tensor(out=actl[:, c, cols], in0=XR[:, c, cols], scalar=gv[:, HM + KC + c:HM + KC + c + 1],
                                               in1=acth[:, c, cols].bitcast(F32), op0=ALU.mult, op1=ALU.subtract).then_inc(xp_lo, 1)
            dve.wait_ge(rv7_done, NT)
            with dve.Fori(0, KC // 2) as g:
                own.enter(g, 6)
                for v in range(6):
                    j, t = v // 3, v % 3
                    dve.wait_ge(pg_mm, g * 6 + v + 1 + 6)
                    nc.vector.tensor_tensor(gn[:, v % 2, :], BANK[v % 2][:, 0:TW], rv[:, t, :], ALU.mult).then_inc(pgn, 1)
                    dve.wait_ge(sg7, g * 6 + v + 1)
                    own.step(nc.vector.tensor_tensor(gn[:, v % 2, :], gn[:, v % 2, :], BANK[2 + v % 2][:, 0:TW], ALU.mult))
                    dve.wait_ge(yt_mm, g * 2 + j + 1)
                    nc.vector.tensor_tensor(yq[:, j, t * TW:(t + 1) * TW], gn[:, v % 2, :],
                                            XR[:, bass.ds(g * 2 + j, 1), t * TW:(t + 1) * TW].rearrange("p a t -> p (a t)"), ALU.add).then_inc(y7_done, 1)
                own.leave(KC // 2)
            end_phase(dve)

        @block.tensor
        def _(pe):
            def transpose_tile(s, rows, n):
                pe.wait_ge(xn_done, n + 3)
                pe.wait_ge(xlo_done, n + 1)
                for k in range(KC):
                    ins = nc.tensor.transpose(BANK[2 * s + k // 4][:, (k % 4) * P:(k % 4) * P + rows],
                                              xn[0:rows, s, k * P:(k + 1) * P], ident[0:rows, 0:rows])
                ins.then_inc(xt_done, 1)

            pe.wait_ge(consts, 2)
            with pe.Fori(0, NCH // 2) as g:
                for s in range(2):
                    transpose_tile(s, P, 2 * g + s)
            transpose_tile(0, NS, NCH)
            pe.wait_ge(wg_lo, 1)
            pe.wait_ge(xlo_done, XTILES + 2)
            for t in range(NT):
                n = 0
                for k in range(KC):
                    for w, x in ((wgh, acth), (wgh, actl), (wgl, acth)):
                        ins = nc.tensor.matmul(BANK[5 + t][0:GW, 0:TW], w[:, k, :], x[:, k, t * TW:(t + 1) * TW],
                                               start=n == 0, stop=n == 3 * KC - 1)
                        n += 1
            ins.then_inc(gate_mm, 1)

            with pe.Fori(0, GROUPS // 2) as g:
                for half in range(2):
                    pe.wait_ge(w_lo1, g * 2 * PIECES + (half + 1) * PIECES + PIECES)
                    for i in range(XTILES):
                        u = half * XTILES + i
                        rows = trows(i)
                        pe.wait_ge(unit_out, g * 18 + u + 1)
                        n = 0
                        for k in range(KC):
                            for x, w in ((acth, wh1), (acth, wl1), (actl, wh1)):
                                ins = nc.tensor.matmul(BANK[u % 3][0:rows, :], x[:, k, i * P:i * P + rows], w[:, half, k, :],
                                                       start=n == 0, stop=n == 3 * KC - 1)
                                n += 1
                        ins.then_inc(unit_mm, 1)
            pe.wait_ge(rows_done, 1)
            for i in range(XTILES):
                bank, c = (3, i) if i < 5 else (4, i - 5)
                rows = trows(i)
                ins = nc.tensor.transpose(BANK[bank][0:rows, c * GW:(c + 1) * GW], rr[:, i * P:i * P + rows], ident[0:GW, 0:GW])
            ins.then_inc(col_mm, 1)
            end_phase(pe)

            begin_phase(pe, 2)
            pe.wait_ge(nst_ld, 16)
            nc.tensor.transpose(pN[:, 0:DB * HM], nst_in[:], ident[0:DB * HM, 0:DB * HM]).then_inc(nst_t, 1)

            def gate_unit(g, f, per, past=0, half=None):
                j, t = f // 3, f % 3
                if half != 1:
                    pe.wait_ge(f_lo, per * g + 3 * past + j + 1 + 3)
                    pe.wait_ge(f_out, 3 * per * g + 9 * past + max(f - 1, 0) + 1)
                ks = range(KC) if half is None else range(half * KC // 2, (half + 1) * KC // 2)
                n = 3 * ks[0]
                for k in ks:
                    for w, x in ((fwh, acth), (fwh, actl), (fwl, acth)):
                        ins = nc.tensor.matmul(BANK[f % 2][:, 0:TW], w[:, j, k, :], x[:, k, t * TW:(t + 1) * TW],
                                               start=n == 0, stop=n == 3 * KC - 1)
                        n += 1
                if half != 0:
                    ins.then_inc(f_mm, 1)

            with pe.Fori(0, HM) as g:
                pe.wait_ge(qkv_in, 96 * g + 96)
                pe.wait_ge(head_done, g + 1)
                for i in range(NCH):
                    nc.tensor.transpose(pA[:, i * P:(i + 1) * P], q_in[:, i, :], ident[:])
                for i in range(NCH):
                    nc.tensor.transpose(pB[:, i * P:(i + 1) * P], k_in[:, i, :], ident[:])
                nc.tensor.transpose(pS[:, 0:NS], q_in[0:NS, NCH, :], ident[0:NS, 0:NS])
                nc.tensor.transpose(pS[:, NS:2 * NS], k_in[0:NS, NCH, :], ident[0:NS, 0:NS]).then_inc(tq_mm, 1)
                gate_unit(g, 0, 3)
                gate_unit(g, 1, 3)
                pe.wait_ge(qkt_done, g + 1)
                pe.wait_ge(qs_done, g + 1)
                for c in range(NCH):
                    nc.tensor.matmul(pA[:, c * P:(c + 1) * P], kT[:, c * P:(c + 1) * P], qT[:, c * P:(c + 1) * P], start=True, stop=True)
                nc.tensor.matmul(pS[0:NS, 0:NS], kT[:, SEQ:], qT[:, SEQ:], start=True, stop=True).then_inc(s_mm, 1)
                pe.wait_ge(kw_done, g + 1)
                for c in range(NCH):
                    nc.tensor.matmul(pB[:, c * P:(c + 1) * P], kw[:, c, :], v_in[:, c, :], start=True, stop=True)
                for c in range(NCH):
                    ins = nc.tensor.matmul(pN[:, c:c + 1], kw[:, c, :], ones[:, 0:1], start=True, stop=True)
                ins.then_inc(u_mm, 1)
                gate_unit(g, 2, 3)
                gate_unit(g, 3, 3)
                pe.wait_ge(sw_done, g + 1)
                pe.wait_ge(c_done, g + 1)
                for c in range(NCH):
                    t = slice(c * P, (c + 1) * P)
                    nc.tensor.matmul(pA[:, t], v_in[:, c, :], sw[:, t], start=True, stop=c == 0)
                    if c > 0:
                        nc.tensor.matmul(pA[:, t], states[:, c - 1, :], qs[:, t], start=False, stop=True)
                    nc.tensor.matmul(pB[:, t], ones[:], sw[:, t], start=True, stop=c == 0)
                    if c > 0:
                        nc.tensor.matmul(pB[:, t], nstates[:, c - 1:c].to_broadcast([P, P]), qs[:, t], start=False, stop=True)
                pe.wait_ge(cs_in, 16 * g + 16)
                nc.tensor.matmul(pS[:, 0:NS], v_in[0:NS, NCH, :], sw[0:NS, SEQ:], start=True, stop=False)
                for b in range(DB):
                    nc.tensor.matmul(pS[:, b * DS:(b + 1) * DS], cst[:, b, :], qs[:, SEQ + b * DS:SEQ + (b + 1) * DS],
                                     start=False, stop=b == DB - 1)
                nc.tensor.matmul(pS[:, NS:2 * NS], ones[0:NS, :], sw[0:NS, SEQ:], start=True, stop=False)
                for b in range(DB):
                    ins = nc.tensor.matmul(pS[:, NS + b * DS:NS + (b + 1) * DS], ncur[:, b:b + 1].to_broadcast([P, P]),
                                           qs[:, SEQ + b * DS:SEQ + (b + 1) * DS], start=False, stop=b == DB - 1)
                ins.then_inc(den_mm, 1)
                gate_unit(g, 4, 3)
                gate_unit(g, 5, 3)
                pe.wait_ge(h_done, g + 1)
                for b in range(DB):
                    nc.tensor.matmul(pA[:, b * DM:(b + 1) * DM], kws[:, b, :], v_in[0:NS, NCH, :], start=True, stop=True)
                for b in range(DB):
                    ins = nc.tensor.matmul(pN[:, NCH + b:NCH + b + 1], kws[:, b, :], ones[0:NS, 0:1], start=True, stop=True)
                ins.then_inc(us_mm, 1)
                for f in range(6, 9):
                    gate_unit(g, f, 3)
            pe.wait_ge(head_done, HM + 1)
            nc.tensor.transpose(pN[0:HM * (DB + 1), 0:P], nout[:], ident[:]).then_inc(n_mm, 1)
            end_phase(pe)

            begin_phase(pe, 3)

            def turn3(g):
                pe.wait_ge(norm3, g + 1)
                pe.wait_ge(nb_done, 8 * g + 8)
                for x, pair in ((qn, pA), (kn, pB)):
                    for i in range(NCH):
                        ins = nc.tensor.transpose(pair[:, i * P:(i + 1) * P], x[:, i, :, :].rearrange("p c d -> p (c d)"), ident[:])
                ins.then_inc(tqk_mm, 1)

            def logits3(g, i):
                pe.wait_ge(nb_done, 8 * g + 8 + (i - 1 if i < 4 and i > 1 else i if i >= 4 else 0))
                out = lg_bank(i)
                q = qst[:, i * P:(i + 1) * P]
                n = (i + 1) * P
                for c in range(0, n, 512):
                    w = min(512, n - c)
                    last = c + w == n
                    nc.tensor.matmul(out[:, c:c + w], q, khh[:, c:c + w], start=True, stop=False)
                    ins = nc.tensor.matmul(out[:, c:c + w], q[0:DH, :], klo[:, c:c + w], start=False, stop=not last)
                    if last:
                        ins = nc.tensor.matmul(out[:, n - P:n], identb[:], maskb[:], start=False, stop=True)
                ins.then_inc(lg_mm, 1)

            def turn_p3(g, i):
                pe.wait_ge(p_done, 8 * g + i + 1)
                if i > 1:
                    pe.wait_ge(pt_lo, 8 * g + (i - 1 if i < 4 else i))
                for j in range(i + 1):
                    ins = nc.tensor.transpose(tp_bank(i)[:, j, :], lg[:, i % 2, j * P:(j + 1) * P], ident[:])
                ins.then_inc(tp_mm, 1)

            def values3(g, m):
                pe.wait_ge(pt_lo, 8 * g + 2 * m + 2)
                if m == 0:
                    pe.wait_ge(v_lo, g + 2)
                    pe.wait_ge(y_done, 2 * g + 1)
                if m == 2:
                    pe.wait_ge(y_done, 2 * g + 2)
                base = m * (m + 1) * 256
                n, total = 0, 3 * (2 * m + 2)
                for j in range(2 * m + 2):
                    skip = P if j == 2 * m + 1 else 0
                    for v, x in ((vh, pth), (vh, ptl), (vl, pth)):
                        ins = nc.tensor.matmul(pC[:, m * 256 + skip:(m + 1) * 256], v[:, j, :],
                                               x[:, base + j * 256 + skip:base + (j + 1) * 256], start=n == 0, stop=n == total - 1)
                        n += 1
                ins.then_inc(pv_mm, 1)

            def pe_head(g):
                gate = lambda f, half: gate_unit(g, f, 1, HM, half)
                turn3(g)
                gate(0, 0)
                pe.wait_ge(qk_lo, g + 1)
                logits3(g, 0)
                logits3(g, 1)
                gate(0, 1)
                logits3(g, 2)
                turn_p3(g, 0)
                logits3(g, 3)
                turn_p3(g, 1)
                turn_p3(g, 2)
                values3(g, 0)
                logits3(g, 4)
                turn_p3(g, 3)
                gate(1, 0)
                logits3(g, 5)
                turn_p3(g, 4)
                values3(g, 1)
                logits3(g, 6)
                turn_p3(g, 5)
                gate(1, 1)
                gate(2, 0)
                logits3(g, 7)
                turn_p3(g, 6)
                values3(g, 2)
                turn_p3(g, 7)
                gate(2, 1)
                values3(g, 3)

            pe.wait_ge(consts, 3)
            with pe.Fori(0, HF - 1) as g:
                pe_head(g)
            pe_head(HF - 1)
            end_phase(pe)

            begin_phase(pe, 4)
            for i in range(XTILES):
                if i % 4 == 0:
                    pe.wait_ge(x4_in[i // 4], 16)
                if i >= 2:
                    pe.wait_ge((x4_a, x4_d)[i % 2], i // 2)
                for k in range(KC):
                    x = xr4[:, i, k * P:(k + 1) * P] if i < NCH else xs4[:, k * P:(k + 1) * P]
                    ins = nc.tensor.transpose((pA, pB)[i % 2][:, k * P:k * P + trows(i)], x,
                                              ident[0:trows(i), 0:trows(i)])
                ins.then_inc(x4_mm, 1)
            pe.wait_ge(x4_a, 5)
            pe.wait_ge(x4_d, 4)
            pe.wait_ge(consts, 4)
            pe.wait_ge(qk4_done, 1)
            for j in range(2):
                for c in range(4):
                    ins = nc.tensor.transpose(BANK[0][:, j * P + c * NS:j * P + (c + 1) * NS],
                                              qk4[:, j, 2 * c:2 * c + 2, :].rearrange("t h d -> t (h d)"), ident[0:NS, 0:NS])
            ins.then_inc(tq4_mm, 1)

            def turn_keys(g, s):
                b, c = s // 4, s % 4
                pe.wait_ge(kt_d if s % 2 else kt_a, 8 * g + s // 2 + 1)
                if c == 0:
                    pe.wait_ge(kpg_in[b], 64 * g + 64)
                for i in range(PAGES):
                    ins = nc.tensor.transpose(kt_bank(s)[:, i * PAGE:(i + 1) * PAGE], kpg[:, b, i, c * P:(c + 1) * P], ident[:])
                ins.then_inc(kt_mm, 1)

            def logits4(g, s):
                b, c = s // 4, s % 4
                n, rows = PAGES * PAGE, slice(b * NS, (b + 1) * NS)
                pe.wait_ge(kt_d if s % 2 else kt_a, 8 * g + s // 2 + 3)
                qb = qz[:, c, b].rearrange("p h t -> p (h t)")
                ins = nc.tensor.matmul(pC[rows, 0:n], qb, ktp[:, c, :], start=c == 0, stop=False)
                if c == 3:
                    for i in range(PAGES):
                        nc.tensor.matmul(pC[rows, 0:(i + 1) * PAGE], lfr[:, b * PAGES + i].rearrange("p h t -> p (h t)"),
                                         sufm[:, (PAGES - 1 - i) * PAGE:], start=False, stop=i == PAGES - 1)
                    new = pC[rows, n:n + NS]
                    for k in range(4):
                        nc.tensor.matmul(new, qz[:, k, b].rearrange("p h t -> p (h t)"), kT4[:, k, :], start=k == 0, stop=False)
                    nc.tensor.matmul(new, lf4[:].rearrange("p h t -> p (h t)"), nmc[:], start=False, stop=False)
                    nc.tensor.matmul(new, sel[:, b].rearrange("p h t -> p (h t)"), maskq[:], start=False, stop=True)
                    ins = nc.tensor.matmul(pC[rows, n + NS:n + NS + 1], lfq[:, b].rearrange("p h t -> p (h t)"), ones[0:NS, 0:1], start=True, stop=True)
                ins.then_inc(l4_mm, 1)

            with pe.Fori(0, DB // GB) as g:
                pe.wait_ge(grp_done, g + 2)
                for s in range(16):
                    turn_keys(g, s)
                    if s >= 2:
                        logits4(g, s - 2)
                logits4(g, 14)
                logits4(g, 15)
                pe.wait_ge(p4_done, g + 2)
                for i in range(PAGES):
                    nc.tensor.transpose(BANK[0][:, i * P:(i + 1) * P], px[:, i * PAGE:(i + 1) * PAGE], ident[:])
                nc.tensor.transpose(BANK[1][0:NS, 0:P], px[:, PAGES * PAGE:], ident[:]).then_inc(tp4_mm, 1)
                pe.wait_ge(pt4_done, g + 1)
                pe.wait_ge(vpg_in, 256 * g + 256)
                for b in range(GB):
                    rows = slice(b * NS, (b + 1) * NS)
                    for i in range(PAGES):
                        nc.tensor.matmul(BANK[0][rows, :], pT4[:, i, rows], vpg[:, b, i, :], start=i == 0, stop=False)
                    ins = nc.tensor.matmul(BANK[0][rows, :], pT4[0:NS, PAGES, rows], v4[:], start=False, stop=True)
                ins.then_inc(o4_mm, 1)
                pe.wait_ge(o4_out, g + 1)
                for c in range(4):
                    ins = nc.tensor.transpose(BANK[1][:, c * P:(c + 1) * P], px[:, c * P:(c + 1) * P], ident[:])
                ins.then_inc(ot4_mm, 1)
            end_phase(pe)

            begin_phase(pe, 5)
            pe.wait_ge(cleared, 1)
            pe.sem_inc(started, 1)

            def product(out, w, x, k_range, start=True, stop=True):
                n, total = 0, 3 * len(k_range)
                for k in k_range:
                    for i, j in ((0, 0), (0, 1), (1, 0)):
                        ins = nc.tensor.matmul(out, w[i](k), x[j](k), start=n == 0, stop=n == total - 1)
                        n += 1
                return ins

            def act_tile(first, t):
                return [lambda k, b=b: b[:, first + k, t * TW:(t + 1) * TW] for b in (acth, actl)]

            def halves(slot, half):
                return [lambda k, b=b: b[:, slot, k * 256 + half * P:k * 256 + (half + 1) * P] for b in (wha, wla)]

            def chunks8(pair, slot):
                return [lambda k, b=b: b[:, slot, k * P:(k + 1) * P] for b in pair]

            pe.wait_ge(y5_lo, 4)
            for c in range(KC):
                if c % 2 == 0:
                    pe.wait_ge(w_split, c // 2 + 3)
                for t in range(NT):
                    u = 3 * c + t
                    if u >= 4:
                        pe.wait_ge(b_done, u + 3)
                    product(BANK[u % 4][:, 0:TW], halves(c // 2 % 2, c % 2), act_tile(4, t), range(4)).then_inc(b_mm, 1)
                if c == 2:
                    for n in range(HM * NT):
                        h, t = n // NT, n % NT
                        pe.wait_ge(hsq, h + 1)
                        if n >= 4:
                            pe.wait_ge(hln, n - 3)
                        nc.tensor.matmul(BANK[4 + n % 4][:, 0:TW], ones[:], rvm[:, h, t * TW:(t + 1) * TW], start=True, stop=True).then_inc(hss_mm, 1)
            pe.wait_ge(b_done, 6 + 3 * KC)
            pe.wait_ge(hm_lo, HM)
            with pe.Fori(0, 2) as g:
                for u in range(12):
                    c, t = u // 3, u % 3
                    if u % 6 == 0:
                        pe.wait_ge(w_split, g * 2 + 4 + c // 2 + 3)
                    pe.wait_ge(t_done, g * 12 + u + 3)
                    product(BANK[u % 4][:, 0:TW], halves(c // 2, c % 2), act_tile(0, t), range(4)).then_inc(a_mm, 1)
            pe.wait_ge(t_lo, 3 * KC)
            pe.wait_ge(rv_zero, 1)
            for t in range(NT):
                nc.tensor.matmul(BANK[4 + t][:, 0:TW], ones[:], rv[:, t, :], start=True, stop=False)
            with pe.Fori(0, KC // 2) as g:
                def sums(j):
                    for t in range(NT):
                        pe.wait_ge(sq5, g * 6 + 3 * j + t + 1)
                        nc.tensor.matmul(BANK[4 + t][:, 0:TW], ones[:], sqt[:, t, :], start=False, stop=False).then_inc(ss5_mm, 1)

                for u in range(6):
                    j, t = u // 3, u % 3
                    if t == 0:
                        pe.wait_ge(w_split, g * 2 + 8 + j + 3)
                    pe.wait_ge(x5_done, g * 6 + u + 1)
                    product(BANK[u % 3][:, 0:TW], chunks8((wha, wla), j), [lambda k, b=b: b[:, k, t * TW:(t + 1) * TW] for b in (th, tl)],
                            range(KC)).then_inc(o_mm, 1)
                    if u == 3:
                        sums(0)
                sums(1)
            for t in range(NT):
                nc.tensor.matmul(BANK[4 + t][:, 0:TW], ones[:], rv[:, t, :], start=False, stop=True).then_inc(ss5_mm, 1)

            pe.wait_ge(xg_lo, 3 * KC)
            def hidden_weights(i):
                return chunks8((wha, wla), i) if i < 2 else chunks8((whb, wlb), i - 2)

            with pe.Fori(0, NFF // 2) as g:
                for v in range(6):
                    j, t = v // 3, v % 3
                    if t == 0:
                        pe.wait_ge(w_split, g * 6 + 16 + 2 * j + 2 + 2)
                    pe.wait_ge(un_done, g * 6 + v + 1)
                    product(BANK[v % 2 * 2][:, 0:TW], hidden_weights(2 * j), act_tile(0, t), range(KC))
                    product(BANK[v % 2 * 2 + 1][:, 0:TW], hidden_weights(2 * j + 1), act_tile(0, t), range(KC)).then_inc(gu_mm, 1)
                pe.wait_ge(w_split, g * 6 + 16 + 6 + 2)
                for u in range(24):
                    t, c = u // KC, u % KC
                    if c == 0:
                        pe.wait_ge(h_lo, g * 6 + 3 + t + 1)
                    pe.wait_ge(x6_done, g * 24 + u + 1)
                    product(BANK[4 + u % 4][:, 0:TW], [lambda k, b=b: b[:, 2 + k, c * P:(c + 1) * P] for b in (whb, wlb)],
                            [lambda k, b=b: b[:, k, t * TW:(t + 1) * TW] for b in (hh, hl)], range(2)).then_inc(dn_mm, 1)

            pe.wait_ge(x6_done, 4 + 12 * NFF)
            pe.wait_ge(p_in, 32)
            for k in range(2):
                for i in range(NCH):
                    nc.tensor.transpose(PAIR[2 * k][:, i * P:(i + 1) * P], pin[:, i, k * P:(k + 1) * P], ident[:])
                nc.tensor.transpose(BANK[k][:, 0:NS], pin[0:NS, NCH, k * P:(k + 1) * P], ident[0:NS, 0:NS]).then_inc(pt7_mm, 1)
            for n in range(NT * KC):
                t, c = n // KC, n % KC
                if n == 2 * KC:
                    pe.wait_ge(pt7_lo, 2)
                pe.wait_ge(sq7, n + 1)
                nc.tensor.matmul(BANK[4 + t][:, 0:TW], ones[:], sqt[:, n % 3, :], start=c == 0, stop=c == KC - 1).then_inc(ss7_mm, 1)
            pe.wait_ge(xp_lo, NT * KC)
            pe.wait_ge(pt7_lo, 2)
            with pe.Fori(0, KC // 2) as g:
                def turn_outputs(j):
                    pe.wait_ge(y7_done, g * 6 + 3 * j + 3 + 2)
                    pe.wait_ge(yt_out, g * 2 + j + 1)
                    for i in range(NCH):
                        nc.tensor.transpose(PAIR[1][:, i * P:(i + 1) * P], yq[:, j, i * P:(i + 1) * P], ident[:])
                    nc.tensor.transpose(BANK[6][0:NS, 0:P], yq[:, j, SEQ:], ident[:]).then_inc(yt_mm, 1)

                for v in range(6):
                    j, t = v // 3, v % 3
                    if t == 0:
                        pe.wait_ge(w_split, g * 2 + 82 + j + 3)
                        pe.wait_ge(pj_split, g * 2 + j + 3)
                    pe.wait_ge(y7_done, g * 6 + v + 1)
                    product(BANK[v % 2][:, 0:TW], chunks8((wha, wla), j), act_tile(0, t), range(KC))
                    product(BANK[2 + v % 2][:, 0:TW], [lambda k, b=b: b[:, j, k, :] for b in (pjh, pjl)],
                            [lambda k, b=b: b[:, k, t * TW:(t + 1) * TW] for b in (pTh, pTl)], range(2)).then_inc(pg_mm, 1)
                turn_outputs(0)
                turn_outputs(1)
            end_phase(pe)


OUTS = [("y_prompt", (1, SEQ, D)), ("y_sample", (DB, DS, D)), ("k_prompt", (1, 1, SEQ, HF, DH)), ("v_prompt", (1, 1, SEQ, HF, DH)),
        ("logf_prompt", (1, 1, SEQ, HF)), ("C_prompt", (1, 1, HM, DM, DM)), ("n_prompt", (1, 1, HM, DM)), ("m_prompt", (1, 1, HM)),
        ("k_sample", (1, DB, DS, HF, DH)), ("v_sample", (1, DB, DS, HF, DH)), ("logf_sample", (1, DB, DS, HF)),
        ("C_sample", (1, DB, HM, DM, DM)), ("n_sample", (1, DB, HM, DM)), ("m_sample", (1, DB, HM))]
SCRATCH = [("zA", (6 * T, W)), ("zT", (20 * P, T)), ("hT", (W, T)), ("yT", (W, T))]
ROWS = ("rows", (3 * HM + HF, T))


def kernel(**inputs):
    import numpy as _np
    import concourse.bacc as _bacc
    from concourse.bass_utils import run_bass_kernel_spmd as _run

    nc = _bacc.Bacc("TRN2", target_bir_lowering=False, num_devices=1)
    arrays, ins, outs = {}, {}, {}
    for name in inputs:
        x = _np.ascontiguousarray(inputs[name])
        arrays[f"in_{name}"] = x
        ins[name] = nc.dram_tensor(f"in_{name}", x.shape, mybir.dt.from_np(x.dtype), kind="ExternalInput").ap()
    for name, shape in OUTS:
        outs[name] = nc.dram_tensor(f"out_{name}", shape, F32, kind="ExternalOutput").ap()
    for name, shape in SCRATCH:
        outs[name] = nc.dram_tensor(f"scratch_{name}", shape, F32, kind="Internal").ap()
    outs["rows"] = nc.dram_tensor("scratch_rows", ROWS[1], F32, kind="Internal").ap()
    program(nc, ins, outs)
    r = _run(nc, [arrays], core_ids=[0])
    return tuple(r.results[0][f"out_{name}"] for name, _ in OUTS)
```
